# Optimizing a Trainium2 kernel written in Bass

```python
import math
import jax, jax.numpy as jnp
from jax import lax
import numpy as np

D_MODEL = 1024
BATCH = 1
SEQ = 256
DEPTH = 2

HEAD_DIM = 64
BLOCK_Q = 128
ROPE_THETA = 500000.0
ROPE_DIMS = HEAD_DIM // 4
EPS = 1e-6
SGU_GROUPS = 4
SGU_WIDTH = SGU_GROUPS * HEAD_DIM
SGU_CHUNK = 128
SB_HEADS = 4
SB_WIDTH = SB_HEADS * HEAD_DIM
NSA_HEADS = 4
NSA_WIDTH = NSA_HEADS * HEAD_DIM
NSA_KV = 6 * HEAD_DIM
CMP_LEN = 32
CMP_STRIDE = 16
CMP_HIDDEN = 256
SEL_LEN = 64
SEL_TOPN = 16
WINDOW = 512
FORCE_SCORE = 1e4
N_BRANCH = 3
IN_WIDTHS = (2 * SGU_WIDTH, SB_WIDTH, SB_WIDTH, SB_WIDTH, NSA_WIDTH, NSA_KV, 3 * NSA_HEADS, N_BRANCH * D_MODEL)
C_IN = sum(IN_WIDTHS)
IN_SPLITS = tuple(int(v) for v in np.cumsum(IN_WIDTHS)[:-1])
D_FF = 2752
N_EXPERTS = 8
TOP_K = 2
D_FF_EXPERT = 3584
MOE_TOKEN_BLOCK = 512

kernel_name = "hybrid_sgu_stickbreak_nsa_moe"

def rmsnorm(x, g):
    xf = x.astype(jnp.float32)
    y = xf * lax.rsqrt(jnp.mean(xf * xf, axis=-1, keepdims=True) + EPS)
    return (y * g.astype(jnp.float32)).astype(x.dtype)

def rope_tables(s):
    inv_freq = ROPE_THETA ** (-jnp.arange(0, ROPE_DIMS, 2, dtype=jnp.float32) / ROPE_DIMS)
    ang = jnp.arange(s, dtype=jnp.float32)[:, None] * inv_freq[None, :]
    return jnp.cos(ang), jnp.sin(ang)

def rope_partial(x, cos, sin):
    half = ROPE_DIMS // 2
    xr = x[..., :ROPE_DIMS].astype(jnp.float32)
    x1, x2 = xr[..., :half], xr[..., half:]
    c, s = cos[None, :, None, :], sin[None, :, None, :]
    rot = jnp.concatenate([x1 * c - x2 * s, x2 * c + x1 * s], axis=-1).astype(x.dtype)
    return jnp.concatenate([rot, x[..., ROPE_DIMS:]], axis=-1)

def masked_softmax(s, mask, axis=-1):
    s = jnp.where(mask, s, -jnp.inf)
    m = jnp.max(s, axis=axis, keepdims=True)
    m = jnp.where(jnp.isfinite(m), m, 0.0)
    p = jnp.exp(s - m)
    d = jnp.sum(p, axis=axis, keepdims=True)
    return p / jnp.where(d > 0, d, 1.0)

def to_blocks(t, nb):
    return jnp.moveaxis(t.reshape(t.shape[0], nb, BLOCK_Q, *t.shape[2:]), 1, 0)

def from_blocks(t):
    t = jnp.moveaxis(t, 0, 1)
    return t.reshape(t.shape[0], t.shape[1] * t.shape[2], *t.shape[3:])

def sgu_mixer(z, norm_g, w_s, b_s):
    b, s, _ = z.shape
    z = jax.nn.gelu(z)
    u, v = jnp.split(z, 2, axis=-1)
    v = rmsnorm(v, norm_g)
    v = v.reshape(b, s // SGU_CHUNK, SGU_CHUNK, SGU_GROUPS, HEAD_DIM)
    w = jnp.where(jnp.tril(jnp.ones((SGU_CHUNK, SGU_CHUNK), bool)), w_s, 0.0).astype(v.dtype)
    mix = jnp.einsum('gts,bcsgd->bctgd', w, v) + b_s.T[:, :, None].astype(v.dtype)
    return u * mix.reshape(b, s, SGU_WIDTH)

def stick_breaking(q, k, v):
    b, s, h, d = q.shape
    nb = s // BLOCK_Q
    scale = d ** -0.5
    kpos = jnp.arange(s)

    def block(args):
        qi, i = args
        qpos = i * BLOCK_Q + jnp.arange(BLOCK_Q)
        mask = kpos[None, :] < qpos[:, None]
        z = jnp.einsum('bthd,bshd->bhts', qi, k).astype(jnp.float32) * scale
        log_beta = jax.nn.log_sigmoid(z)
        log_1m = jnp.where(mask, jax.nn.log_sigmoid(-z), 0.0)
        between = lax.cumsum(log_1m, axis=3, reverse=True) - log_1m
        a = jnp.where(mask, jnp.exp(log_beta + between), 0.0)
        return jnp.einsum('bhts,bshd->bthd', a.astype(v.dtype), v)

    out = lax.map(block, (to_blocks(q, nb), jnp.arange(nb)))
    return from_blocks(out).reshape(b, s, h * d)

def compress(t, pos_emb, w1, w2):
    b, s, d = t.shape
    m = (s - CMP_LEN) // CMP_STRIDE + 1
    idx = jnp.arange(m)[:, None] * CMP_STRIDE + jnp.arange(CMP_LEN)[None, :]
    blocks = t[:, idx] + pos_emb.astype(t.dtype)
    hid = jax.nn.gelu(blocks.reshape(b, m, CMP_LEN * d) @ w1)
    return hid @ w2

def nsa(q, k_cmp, v_cmp, k_slc, v_slc, k_win, v_win, gates, cmp_pos, cmp_w1, cmp_w2):
    b, s, h, d = q.shape
    nb = s // BLOCK_Q
    scale = d ** -0.5
    kc = compress(k_cmp, cmp_pos[0], cmp_w1[0], cmp_w2[0])
    vc = compress(v_cmp, cmp_pos[1], cmp_w1[1], cmp_w2[1])
    m = kc.shape[1]
    cmp_end = jnp.arange(m) * CMP_STRIDE + CMP_LEN - 1
    ns = s // SEL_LEN
    n_top = min(SEL_TOPN, ns)
    ks_blocks = k_slc.reshape(b, ns, SEL_LEN, d)
    vs_blocks = v_slc.reshape(b, ns, SEL_LEN, d)
    cs = (jnp.arange(m) * CMP_STRIDE)[:, None]
    ss = (jnp.arange(ns) * SEL_LEN)[None, :]
    overlap = jnp.clip(jnp.minimum(cs + CMP_LEN, ss + SEL_LEN) - jnp.maximum(cs, ss), 0).astype(jnp.float32) / CMP_LEN
    blk_ids = jnp.arange(ns)
    kw_pad = jnp.pad(k_win, ((0, 0), (WINDOW, 0), (0, 0)))
    vw_pad = jnp.pad(v_win, ((0, 0), (WINDOW, 0), (0, 0)))
    gather = jax.vmap(lambda blk, ix: blk[ix])

    def block(args):
        qi, gi, i = args
        qpos = i * BLOCK_Q + jnp.arange(BLOCK_Q)
        s_cmp = jnp.einsum('bthd,bmd->bhtm', qi, kc).astype(jnp.float32) * scale
        p_cmp = masked_softmax(s_cmp, cmp_end[None, :] <= qpos[:, None])
        o_cmp = jnp.einsum('bhtm,bmd->bthd', p_cmp.astype(vc.dtype), vc)
        imp = jnp.einsum('bhtm,mj->btj', p_cmp, overlap)
        valid = (blk_ids * SEL_LEN)[None, :] <= qpos[:, None]
        forced = (blk_ids[None, :] == 0) | (blk_ids[None, :] == (qpos // SEL_LEN)[:, None])
        score = jnp.where(valid, imp + jnp.where(forced, FORCE_SCORE, 0.0), -jnp.inf)
        top_val, top_idx = lax.top_k(score, n_top)
        sel_ok = jnp.isfinite(top_val)
        kg = gather(ks_blocks, top_idx)
        vg = gather(vs_blocks, top_idx)
        s_slc = jnp.einsum('bthd,btkld->bhtkl', qi, kg).astype(jnp.float32) * scale
        tok_pos = top_idx[..., None] * SEL_LEN + jnp.arange(SEL_LEN)
        m_slc = sel_ok[..., None] & (tok_pos <= qpos[None, :, None, None])
        p_slc = masked_softmax(s_slc.reshape(b, h, BLOCK_Q, n_top * SEL_LEN),
                               m_slc.reshape(b, 1, BLOCK_Q, n_top * SEL_LEN))
        o_slc = jnp.einsum('bhtkl,btkld->bthd', p_slc.reshape(s_slc.shape).astype(vg.dtype), vg)
        kw = lax.dynamic_slice_in_dim(kw_pad, i * BLOCK_Q, WINDOW + BLOCK_Q, axis=1)
        vw = lax.dynamic_slice_in_dim(vw_pad, i * BLOCK_Q, WINDOW + BLOCK_Q, axis=1)
        kwpos = i * BLOCK_Q - WINDOW + jnp.arange(WINDOW + BLOCK_Q)
        m_win = (kwpos[None, :] <= qpos[:, None]) & (kwpos[None, :] > qpos[:, None] - WINDOW) & (kwpos[None, :] >= 0)
        s_win = jnp.einsum('bthd,bsd->bhts', qi, kw).astype(jnp.float32) * scale
        p_win = masked_softmax(s_win, m_win)
        o_win = jnp.einsum('bhts,bsd->bthd', p_win.astype(vw.dtype), vw)
        return gi[..., 0:1] * o_cmp + gi[..., 1:2] * o_slc + gi[..., 2:3] * o_win

    out = lax.map(block, (to_blocks(q, nb), to_blocks(gates, nb), jnp.arange(nb)))
    return from_blocks(out).reshape(b, s, h * d)

def hybrid_mixer(hn, w_in, sgu_norm_g, sgu_w, sgu_b, cmp_pos, cmp_w1, cmp_w2, w_branch, w_out, cos, sin):
    b, s, _ = hn.shape
    proj = hn @ w_in
    a_in, sb_q, sb_k, sb_v, c_q, c_kv, c_g, br_g = jnp.split(proj, IN_SPLITS, axis=-1)
    heads = lambda t, n: t.reshape(b, s, n, HEAD_DIM)
    y_a = sgu_mixer(a_in, sgu_norm_g, sgu_w, sgu_b)
    y_b = stick_breaking(heads(sb_q, SB_HEADS), heads(sb_k, SB_HEADS), heads(sb_v, SB_HEADS))
    q = rope_partial(heads(c_q, NSA_HEADS), cos, sin)
    k_cmp, v_cmp, k_slc, v_slc, k_win, v_win = jnp.split(c_kv, 6, axis=-1)
    rk = lambda t: rope_partial(t[:, :, None, :], cos, sin)[:, :, 0, :]
    nsa_g = jax.nn.sigmoid(c_g.astype(jnp.float32)).reshape(b, s, NSA_HEADS, 3).astype(hn.dtype)
    y_c = nsa(q, rk(k_cmp), v_cmp, rk(k_slc), v_slc, rk(k_win), v_win, nsa_g, cmp_pos, cmp_w1, cmp_w2)
    g = jax.nn.sigmoid(br_g.astype(jnp.float32)).reshape(b, s, N_BRANCH, D_MODEL).astype(hn.dtype)
    merged = (g[:, :, 0] * (y_a @ w_branch[0]) + g[:, :, 1] * (y_b @ w_branch[1])
              + g[:, :, 2] * (y_c @ w_branch[2]))
    return merged @ w_out

def swiglu(h, w_gate, w_up, w_down):
    return (jax.nn.silu(h @ w_gate) * (h @ w_up)) @ w_down

def moe_swiglu(h, router_w, w_gate, w_up, w_down):
    b, s, d = h.shape
    n = b * s
    chunk = MOE_TOKEN_BLOCK if n % MOE_TOKEN_BLOCK == 0 else BLOCK_Q
    logits = (h @ router_w).astype(jnp.float32)
    top_val, top_idx = lax.top_k(logits, TOP_K)
    wts = jax.nn.softmax(top_val, axis=-1)
    gate = jnp.sum(jax.nn.one_hot(top_idx, N_EXPERTS, dtype=jnp.float32) * wts[..., None], axis=-2)

    def run(args):
        xc, gc = args
        a = jnp.einsum('nd,edf->nef', xc, w_gate)
        u = jnp.einsum('nd,edf->nef', xc, w_up)
        hid = jax.nn.silu(a) * u * gc[..., None].astype(xc.dtype)
        return jnp.einsum('nef,efd->nd', hid, w_down)

    out = lax.map(run, (h.reshape(n // chunk, chunk, d), gate.reshape(n // chunk, chunk, N_EXPERTS)))
    return out.reshape(b, s, d)

def setup_inputs(seed: int = 0) -> dict:
    key = jax.random.key(seed)
    ks = jax.random.split(key, 24)
    n_dense = (DEPTH + 1) // 2
    n_moe = DEPTH // 2
    nrm = lambda k, shape, sc: jax.random.normal(k, shape, jnp.float32) * sc
    return {
        "x": nrm(ks[0], (BATCH, SEQ, D_MODEL), 1.0),
        "norm1_g": 1.0 + nrm(ks[1], (DEPTH, D_MODEL), 0.02),
        "w_in": nrm(ks[2], (DEPTH, D_MODEL, C_IN), D_MODEL ** -0.5),
        "sgu_norm_g": 1.0 + nrm(ks[3], (DEPTH, SGU_WIDTH), 0.02),
        "sgu_w": nrm(ks[4], (DEPTH, SGU_GROUPS, SGU_CHUNK, SGU_CHUNK), SGU_CHUNK ** -0.5),
        "sgu_b": 1.0 + nrm(ks[5], (DEPTH, SGU_GROUPS, SGU_CHUNK), 0.1),
        "cmp_pos": nrm(ks[6], (DEPTH, 2, CMP_LEN, HEAD_DIM), 0.02),
        "cmp_w1": nrm(ks[7], (DEPTH, 2, CMP_LEN * HEAD_DIM, CMP_HIDDEN), (CMP_LEN * HEAD_DIM) ** -0.5),
        "cmp_w2": nrm(ks[8], (DEPTH, 2, CMP_HIDDEN, HEAD_DIM), CMP_HIDDEN ** -0.5),
        "w_branch": nrm(ks[9], (DEPTH, N_BRANCH, SB_WIDTH, D_MODEL), SB_WIDTH ** -0.5),
        "w_out": nrm(ks[10], (DEPTH, D_MODEL, D_MODEL), D_MODEL ** -0.5),
        "norm2_g": 1.0 + nrm(ks[11], (DEPTH, D_MODEL), 0.02),
        "ffn_w_gate": nrm(ks[12], (n_dense, D_MODEL, D_FF), D_MODEL ** -0.5),
        "ffn_w_up": nrm(ks[13], (n_dense, D_MODEL, D_FF), D_MODEL ** -0.5),
        "ffn_w_down": nrm(ks[14], (n_dense, D_FF, D_MODEL), D_FF ** -0.5),
        "router_w": nrm(ks[15], (n_moe, D_MODEL, N_EXPERTS), D_MODEL ** -0.5),
        "moe_w_gate": nrm(ks[16], (n_moe, N_EXPERTS, D_MODEL, D_FF_EXPERT), D_MODEL ** -0.5),
        "moe_w_up": nrm(ks[17], (n_moe, N_EXPERTS, D_MODEL, D_FF_EXPERT), D_MODEL ** -0.5),
        "moe_w_down": nrm(ks[18], (n_moe, N_EXPERTS, D_FF_EXPERT, D_MODEL), D_FF_EXPERT ** -0.5),
        "final_norm_g": 1.0 + nrm(ks[19], (D_MODEL,), 0.02),
    }

def reference(x, norm1_g, w_in, sgu_norm_g, sgu_w, sgu_b, cmp_pos, cmp_w1, cmp_w2, w_branch, w_out,
              norm2_g, ffn_w_gate, ffn_w_up, ffn_w_down, router_w, moe_w_gate, moe_w_up, moe_w_down,
              final_norm_g):
    cos, sin = rope_tables(x.shape[1])
    h = x
    for layer in range(DEPTH):
        hn = rmsnorm(h, norm1_g[layer])
        h = h + hybrid_mixer(hn, w_in[layer], sgu_norm_g[layer], sgu_w[layer], sgu_b[layer], cmp_pos[layer],
                             cmp_w1[layer], cmp_w2[layer], w_branch[layer], w_out[layer], cos, sin)
        hn = rmsnorm(h, norm2_g[layer])
        j = layer // 2
        if layer % 2 == 0:
            h = h + swiglu(hn, ffn_w_gate[j], ffn_w_up[j], ffn_w_down[j])
        else:
            h = h + moe_swiglu(hn, router_w[j], moe_w_gate[j], moe_w_up[j], moe_w_down[j])
    return rmsnorm(h, final_norm_g)


_drawn_inputs = setup_inputs


def setup_inputs(seed=0):
    import zlib

    import numpy as np

    out = dict(_drawn_inputs(seed))
    spreads = {}
    factors = {'sgu_norm_g': 3.771, 'cmp_pos': 3.598, 'final_norm_g': 2.834}
    for name, (base, spread) in spreads.items():
        noise = np.random.default_rng([zlib.crc32(name.encode()), seed]).standard_normal(out[name].shape)
        drawn = base * np.exp(spread * noise) if base else spread * noise
        out[name] = __import__('jax').numpy.asarray(drawn.astype(out[name].dtype))
    for name, factor in factors.items():
        out[name] = (out[name] * factor).astype(out[name].dtype)
    return out
```

```python
from contextlib import ExitStack

import concourse.bass as bass
from concourse import mybir

F32 = mybir.dt.float32
F32R = mybir.dt.float32r
I32 = mybir.dt.int32
U32 = mybir.dt.uint32
ALU = mybir.AluOpType
ACT = mybir.ActivationFunctionType
AX_X = mybir.AxisListType.X

P = 128
LAYERS = 2
D = 1024
T = 256
TT = T // P
KC = D // P
HD = 64
HEADS = 4
A0, SB0, TOK0, CKV0, GATE0 = 0, 512, 1024, 1536, 1932
CKV_N = GATE0 - CKV0
PT_N = 512 + CKV_N
CMP_M = (T - 32) // 16 + 1
CMP_C = 32 * HD // P
D_FF = 2752
FG = 256
FFN_FULL = D_FF // FG
FT = D_FF - FFN_FULL * FG
EXPERTS = 8
D_E = 3584
STEPS = D_E // 512
CAPACITY = P
EPS = 1e-6
NEG = -1e30
SCALE = HD ** -0.5

UNIT = 2048
RAW = 6
SPLIT = 3
MIX_UNITS = 27
FFN_UNITS = 3 * FFN_FULL + 4
PER_EXPERT = 6 * STEPS
FFN_U = MIX_UNITS
MIX1_U = FFN_U + FFN_UNITS
MOE_U = MIX1_U + MIX_UNITS
MOE_UNITS = EXPERTS * PER_EXPERT


def bc(ap, axis, n):
    a = ap.unsqueeze(axis)
    shape = list(a.shape)
    shape[axis] = n
    return a.broadcast_to(shape)


def hybrid_trunk(nc, x, norm1_g, w_in, sgu_norm_g, sgu_w, sgu_b, cmp_pos, cmp_w1, cmp_w2, w_branch, w_out,
                 norm2_g, ffn_w_gate, ffn_w_up, ffn_w_down, router_w, moe_w_gate, moe_w_up, moe_w_down,
                 final_norm_g, rope, out):
    ctx = ExitStack()
    with ctx:
        def sb(name, shape, dt=F32):
            return ctx.enter_context(nc.sbuf_tensor(name, shape, dt))

        def sem(name):
            return ctx.enter_context(nc.semaphore(name))

        raw = sb("raw", [P, RAW, UNIT])
        w_hi = sb("w_hi", [P, SPLIT, UNIT], F32R)
        w_lo = sb("w_lo", [P, SPLIT, UNIT], F32R)
        h = sb("h", [P, TT, D])
        hn = sb("hn", [P, TT, D])
        xT_hi = sb("xT_hi", [P, KC, T], F32R)
        xT_lo = sb("xT_lo", [P, KC, T], F32R)
        gain = sb("gain", [P, D])
        ident = sb("ident", [P, P])
        ones = sb("ones", [P, P])
        later = sb("later", [P, P])
        before = sb("before", [P, P])
        causal = sb("causal", [P, 3, P])
        cmp_mask = sb("cmp_mask", [P, TT, CMP_M])
        rope_sb = sb("rope_sb", [P, TT, 3, 8])
        eps = sb("eps", [P, 1])
        ssq = sb("ssq", [P, TT])
        rstd = sb("rstd", [P, TT])
        psum = ctx.enter_context(nc.psum_tensor("psum", [P, 8, 512], F32))

        with ExitStack() as own:
            def mb(name, shape, dt=F32):
                return own.enter_context(nc.sbuf_tensor(name, shape, dt))
            gates = mb("gates", [P, 24, T])
            tok = mb("tok", [P, TT, PT_N])
            sbT = mb("sbT", [P, 4, T])
            uv = mb("uv", [P, TT, 512])
            qT = mb("qT", [P, 2, T])
            kT = mb("kT", [P, 4, T])
            att = mb("att", [P, HEADS, 384])
            y_hi = mb("y_hi", [P, 3, 2, T], F32R)
            y_lo = mb("y_lo", [P, 3, 2, T], F32R)
            sgu_T = mb("sgu_T", [P, 4, P])
            sgu_g = mb("sgu_g", [P, T])
            small = mb("small", [P, 256])
            posT = mb("posT", [P, 64])
            biasT = mb("biasT", [P, LAYERS, 4])
            w2k = mb("w2k", [P, 2, P])
            w2v = mb("w2v", [P, 2, HD])
            hid_cT = mb("hid_cT", [P, 2, 2, CMP_M])
            kcT = mb("kcT", [P, CMP_M])
            vc = mb("vc", [CMP_M, HD])
            blk = mb("blk", [P, 2, CMP_C, CMP_M])
            pc = mb("pc", [P, 2, TT, 2, CMP_M])
        with ExitStack() as own:
            def mb(name, shape, dt=F32):
                return own.enter_context(nc.sbuf_tensor(name, shape, dt))
            f_silu = mb("f_silu", [P, 512])
            f_hid = mb("f_hid", [P, 512])
            f_hi = mb("f_hi", [P, 2, 2, T], F32R)
            f_lo = mb("f_lo", [P, 2, 2, T], F32R)
        with ExitStack() as own:
            def mb(name, shape, dt=F32):
                return own.enter_context(nc.sbuf_tensor(name, shape, dt))
            pick = mb("pick", [P, EXPERTS + 1, TT, P])
            spread = mb("spread", [P, EXPERTS, T])
            spread_e = mb("spread_e", [P, T])
            sel_hi = mb("sel_hi", [P, KC, P], F32R)
            sel_lo = mb("sel_lo", [P, KC, P], F32R)
            y_e = mb("y_e", [P, D])
            e_silu = mb("e_silu", [P, 512])
            e_hid = mb("e_hid", [P, 512])
            eT_hi = mb("eT_hi", [P, 4, P], F32R)
            eT_lo = mb("eT_lo", [P, 4, P], F32R)
            xTf = mb("xTf", [P, KC, T])
            gated = mb("gated", [P, EXPERTS, TT, P])
            slot_no = mb("slot_no", [P, P])
            rw = mb("rw", [P, KC, EXPERTS])
            lg = mb("lg", [P, TT, EXPERTS])
            top_v = mb("top_v", [P, TT, 8])
            top_i = mb("top_i", [P, TT, 8], U32)
            top_f = mb("top_f", [P, TT, 2])
            ex = mb("ex", [P, TT, 2])
            hit = mb("hit", [P, 2, TT, EXPERTS])
            gate = mb("gate", [P, TT, EXPERTS])
            chosen = mb("chosen", [P, TT, EXPERTS])
            place = mb("place", [P, TT, EXPERTS])
            most = mb("most", [P, 1])
            most_i = mb("most_i", [P, 1], I32)

        scr = hn[:, :, :].rearrange("p t d -> p (t d)")
        dup = scr[:, 0:1024].rearrange("p (t k c) -> p t k c", t=TT, k=4)
        sc = scr[:, 0:1536].rearrange("p (h c) -> p h c", h=HEADS)
        hid_c = scr[0:CMP_M, 1536:2048].rearrange("p (v c) -> p v c", v=2)
        w1 = gates[:, 0:16, :]
        sgu_raw = gates[:, 22:24, :].rearrange("p a (g s) -> p (a g) s", g=2)
        pos_b, sb_b = gates[0:64, 16, 0:P], gates[0:8, 17, 0:P]
        ysum = kT[:, 0:2, :]

        landed = [sem(f"landed{n}") for n in range(RAW)]
        hi_ready, lo_ready, unit_used = sem("hi_ready"), sem("lo_ready"), sem("unit_used")
        x_landed, rope_landed, rw_landed = sem("x_landed"), sem("rope_landed"), sem("rw_landed")
        posb_landed, w2_landed, sguw_landed, sgug_landed = sem("posb_landed"), sem("w2_landed"), sem("sguw_landed"), sem("sgug_landed")
        w1_landed = sem("w1_landed")
        gain_landed = sem("gain_landed")
        consts, pool_step = sem("consts"), sem("pool_step")
        sq_ready, rt_ready, hn_ready, hnT_done, xT_hi_ready, xT_ready = (
            sem("sq_ready"), sem("rt_ready"), sem("hn_ready"), sem("hnT_done"), sem("xT_hi_ready"), sem("xT_ready"))
        dve_step, act_step = sem("dve_step"), sem("act_step")
        sbT_ready, tokA_ready, tokB_ready, uv_ready = sem("sbT_ready"), sem("tokA_ready"), sem("tokB_ready"), sem("uv_ready")
        roped, dup_ready, kTp_done, kT_ready = sem("roped"), sem("dup_ready"), sem("kTp_done"), sem("kT_ready")
        qTp_done, qT_ready, sguTp_done, sguT_ready, sguT_cut = sem("qTp_done"), sem("qT_ready"), sem("sguTp_done"), sem("sguT_ready"), sem("sguT_cut")
        gate_copied, gates_ready = sem("gate_copied"), sem("gates_ready")
        z_done, zs_ready, soft_ready, lb_ready, sp_ready, sp_cut = sem("z_done"), sem("zs_ready"), sem("soft_ready"), sem("lb_ready"), sem("sp_ready"), sem("sp_cut")
        btw_done, arg_ready, aT_exp, aT_ready, yb_done, yb_hi = sem("btw_done"), sem("arg_ready"), sem("aT_exp"), sem("aT_ready"), sem("yb_done"), sem("yb_hi")
        small_T, small_T_ready = sem("small_T"), sem("small_T_ready")
        blk_ready, ck_done, hc_ready, hcT_done, hcT_ready, kc_done, kc_ready = (
            sem("blk_ready"), sem("ck_done"), sem("hc_ready"), sem("hcT_done"), sem("hcT_ready"), sem("kc_done"), sem("kc_ready"))
        vsq_ready, vrt_ready, vn_ready, mix_done, ya_ready, yaT_done, ya_hi = (
            sem("vsq_ready"), sem("vrt_ready"), sem("vn_ready"), sem("mix_done"), sem("ya_ready"), sem("yaT_done"), sem("ya_hi"))
        gsig = sem("gsig")
        s_done, sm_ready, p_exp, p_ready, pT_done, pT_ready, av_done, av_added, yc_ready, yc_hi, y_ready = (
            sem("s_done"), sem("sm_ready"), sem("p_exp"), sem("p_ready"), sem("pT_done"), sem("pT_ready"),
            sem("av_done"), sem("av_added"), sem("yc_ready"), sem("yc_hi"), sem("y_ready"))
        br_done, br_used, merged, mg_hi, mg_ready, h_mixed = (
            sem("br_done"), sem("br_used"), sem("merged"), sem("mg_hi"), sem("mg_ready"), sem("h_mixed"))
        f_silu_ready, f_hid_ready, f_hi_ready, f_lo_ready, h_ffn = (
            sem("f_silu_ready"), sem("f_hid_ready"), sem("f_hi_ready"), sem("f_lo_ready"), sem("h_ffn"))
        xTf_ready, lg_done, dv_ready, ex_ready, chosen_ready, pos_done, most_ready = (
            sem("xTf_ready"), sem("lg_done"), sem("dv_ready"), sem("ex_ready"), sem("chosen_ready"), sem("pos_done"), sem("most_ready"))
        pick_ready, gated_ready, spreadT_done, spread_ready, spread_e_ready = (
            sem("pick_ready"), sem("gated_ready"), sem("spreadT_done"), sem("spread_ready"), sem("spread_e_ready"))
        gather_done, sel_hi_ready, sel_ready = sem("gather_done"), sem("sel_hi_ready"), sem("sel_ready")
        e_silu_ready, e_hid_ready, e_T, eT_hi_ready, eT_ready = (
            sem("e_silu_ready"), sem("e_hid_ready"), sem("e_T"), sem("eT_hi_ready"), sem("eT_ready"))
        y_e_ready, scatter_done, h_added, rest_step = (
            sem("y_e_ready"), sem("scatter_done"), sem("h_added"), sem("rest_step"))
        out_ready, stored = sem("out_ready"), sem("stored")

        def load_unit(sp, u, src, i=0, every=0, parts=P):
            if u >= RAW:
                sp.wait_ge(lo_ready, i * every + (u - RAW + 1))
            n = 1
            for s in src.shape[1:]:
                n *= s
            dst = raw[0:parts, u % RAW, 0:n]
            if len(src.shape) == 3:
                dst = dst.rearrange("p (a b) -> p a b", a=src.shape[1])
            sp.dma_start(dst, src).then_inc(landed[u % RAW], 16)

        def split_hi(act, u, i=0, every=0, parts=P, n=UNIT):
            act.wait_ge(landed[u % RAW], i * (every // RAW * 16) + 16 * (u // RAW + 1))
            if u >= SPLIT:
                act.wait_ge(unit_used, i * every + (u - SPLIT + 1))
            nc.scalar.activation(w_hi[0:parts, u % SPLIT, 0:n], raw[0:parts, u % RAW, 0:n], ACT.Copy).then_inc(hi_ready, 1)

        def split_lo(dve, u, i=0, every=0, parts=P, n=UNIT):
            dve.wait_ge(hi_ready, i * every + (u + 1))
            if u >= SPLIT:
                dve.wait_ge(unit_used, i * every + (u - SPLIT + 1))
            nc.vector.tensor_tensor(w_lo[0:parts, u % SPLIT, 0:n], raw[0:parts, u % RAW, 0:n],
                                    w_hi[0:parts, u % SPLIT, 0:n].bitcast(F32), ALU.subtract).then_inc(lo_ready, 1)

        def unit(pe, u, a, i=0, every=0, parts=P, n=UNIT):
            pe.wait_ge(lo_ready, i * every + (u + 1))
            return [w[0:parts, u % SPLIT, 0:n].rearrange("p (a b) -> p a b", a=a) for w in (w_hi, w_lo)]

        def mm3(o, lhs, rhs, start, stop):
            nc.tensor.matmul(o, lhs[0], rhs[0], start=start, stop=False)
            nc.tensor.matmul(o, lhs[0], rhs[1], start=False, stop=False)
            return nc.tensor.matmul(o, lhs[1], rhs[0], start=False, stop=stop)

        def odd_shape(u):
            for base in (0, MIX1_U):
                if u - base in (4, 5):
                    return {"n": 4 * CKV_N}
            if u in (FFN_U + 3 * FFN_FULL - 1, FFN_U + 3 * FFN_FULL):
                return {"n": KC * FT}
            if u == FFN_U + 3 * FFN_FULL + 2:
                return {"n": D}
            if u == FFN_U + 3 * FFN_FULL + 3:
                return {"n": D, "parts": FT - P}
            return {}

        xT = (xT_hi, xT_lo)
        block = ctx.enter_context(nc.Block())

        @block.sync
        def _(sp):
            sp.dma_start(h[:, :, :], x[0].rearrange("(t p) d -> p t d", p=P)).then_inc(x_landed, 16)

            def mixer_units(L, base):
                w = w_in[L].rearrange("(k p) n -> p k n", p=P)
                for n in range(2):
                    load_unit(sp, base + n, w[:, :, SB0 + n * 256:SB0 + (n + 1) * 256])
                for n, (c, width) in enumerate(((TOK0, 512), (CKV0, CKV_N), (A0, 512))):
                    for half in range(2):
                        load_unit(sp, base + 2 + 2 * n + half, w[:, 4 * half:4 * half + 4, c:c + width])
                for n in range(12):
                    c = GATE0 + ((n + 8) % 12) * 256
                    load_unit(sp, base + 8 + n, w[:, :, c:c + 256])
                for n in range(3):
                    load_unit(sp, base + 20 + n, w_branch[L, n].rearrange("(k p) n -> p k n", p=P))
                for n in range(4):
                    load_unit(sp, base + 23 + n, w_out[L].rearrange("(k p) n -> p k n", p=P)[:, 2 * n:2 * n + 2, :])

            mixer_units(0, 0)
            fg, fu = (w[0].rearrange("(k p) n -> p k n", p=P) for w in (ffn_w_gate, ffn_w_up))

            def ffn_down(g):
                return ffn_w_down[0, bass.ds(g * FG, FG), :].rearrange("(k p) n -> p k n", p=P)
            load_unit(sp, FFN_U, fg[:, :, 0:FG])
            load_unit(sp, FFN_U + 1, fu[:, :, 0:FG])
            with sp.Fori(0, 4) as i:
                for b in range(2):
                    u = FFN_U + 2 + 3 * b
                    load_unit(sp, u, fg[:, :, bass.ds(i * (2 * FG) + (b + 1) * FG, FG)], i, 6)
                    load_unit(sp, u + 1, fu[:, :, bass.ds(i * (2 * FG) + (b + 1) * FG, FG)], i, 6)
                    load_unit(sp, u + 2, ffn_down(i * 2 + b), i, 6)
            u, c = FFN_U + 26, 9 * FG
            load_unit(sp, u, fg[:, :, c:c + FG])
            load_unit(sp, u + 1, fu[:, :, c:c + FG])
            load_unit(sp, u + 2, ffn_down(8))
            load_unit(sp, u + 3, fg[:, :, D_FF - FT:D_FF])
            load_unit(sp, u + 4, fu[:, :, D_FF - FT:D_FF])
            load_unit(sp, u + 5, ffn_down(9))
            load_unit(sp, u + 6, ffn_w_down[0, D_FF - FT:D_FF - FT + P, :])
            load_unit(sp, u + 7, ffn_w_down[0, D_FF - FT + P:D_FF, :], parts=FT - P)
            mixer_units(1, MIX1_U)

            def expert_units(base, i, first):
                eg, eu = (w[0, i if first else bass.ds(i, 1)].rearrange("(k p) n -> p k n" if first else "a (k p) n -> p (a k) n", p=P)
                          for w in (moe_w_gate, moe_w_up))

                def down(e, j, u, k):
                    for half in range(2):
                        r = 512 * j + 256 * half
                        src = moe_w_down[0, bass.ds(e, 1), r:r + 256, :].rearrange("a (k p) n -> p (a k) n", p=P)
                        load_unit(sp, u + half, src, k, PER_EXPERT)
                for j in range(STEPS):
                    shift = 2 if first and j == 0 else 0
                    for n, w in enumerate((eg, eu)):
                        for half in range(2):
                            load_unit(sp, base + 6 * j + shift + 2 * n + half,
                                      w[:, 4 * half:4 * half + 4, 512 * j:512 * j + 512], i, PER_EXPERT)
                    if j:
                        down(i, j - 1, base + 6 * j + 4, i)
                    elif not first:
                        down(i - 1, STEPS - 1, base + 4, i)

            def expert_stream(start):
                expert_units(start - 2, 0, True)
                with sp.Fori(1, EXPERTS) as i:
                    expert_units(start - 2, i, False)
                for half in range(2):
                    r = 512 * (STEPS - 1) + 256 * half
                    load_unit(sp, start + MOE_UNITS - 2 + half,
                              moe_w_down[0, EXPERTS - 1, r:r + 256, :].rearrange("(k p) n -> p k n", p=P))
            expert_stream(MOE_U)
            sp.wait_ge(most_ready, 1)
            with sp.If(sp.value_load(most_i[0:1, 0:1], min_val=0, max_val=T) > CAPACITY):
                expert_stream(MOE_U + MOE_UNITS)
            for t in range(TT):
                sp.wait_ge(out_ready, t + 1)
                sp.dma_start(out[0, t * P:(t + 1) * P, :], hn[:, t, :]).then_inc(stored, 16)
            sp.wait_ge(stored, 16 * TT)

        @block.gpsimd
        def _(pool):
            steps = [0]

            def step(ins):
                steps[0] += 1
                ins.then_inc(pool_step, 1)
                pool.wait_ge(pool_step, steps[0])

            def load_gain(n, vector):
                if n:
                    pool.wait_ge(hn_ready, 2 * n)
                pool.dma_start(gain[:, :], vector.partition_broadcast(P)).then_inc(gain_landed, 16)
            load_gain(0, norm1_g[0])
            pool.dma_start(rope_sb[:, :, :, :], rope.rearrange("(t p) (a b) -> p t a b", p=P, a=3)).then_inc(rope_landed, 16)
            pool.dma_start(pos_b, cmp_pos.rearrange("l v (c a) d -> (l v c) (a d)", a=2)).then_inc(posb_landed, 16)
            pool.dma_start(sb_b, sgu_b.rearrange("l g t -> (l g) t")).then_inc(posb_landed, 16)
            nc.gpsimd.memset(eps[:, :], EPS)
            nc.gpsimd.memset(ident[:, :], 0.0)
            nc.gpsimd.memset(ones[:, :], 1.0)
            nc.gpsimd.memset(later[:, :], 1.0)
            nc.gpsimd.memset(before[:, :], 1.0)
            nc.gpsimd.memset(cmp_mask[:, :, :], 0.0)
            step(nc.gpsimd.memset(causal[:, :, :], 0.0))
            nc.gpsimd.affine_select(out=ident[:, :], in_=ident[:, :], compare_op=ALU.not_equal, fill=1.0, base=0,
                                    pattern=[[-1, P]], channel_multiplier=1)
            nc.gpsimd.affine_select(out=later[:, :], in_=later[:, :], compare_op=ALU.is_gt, fill=0.0, base=0,
                                    pattern=[[-1, P]], channel_multiplier=1)
            nc.gpsimd.affine_select(out=before[:, :], in_=before[:, :], compare_op=ALU.is_gt, fill=0.0, base=0,
                                    pattern=[[1, P]], channel_multiplier=-1)
            nc.gpsimd.affine_select(out=causal[:, 0:3:2, :], in_=causal[:, 0:3:2, :], compare_op=ALU.is_ge, fill=NEG,
                                    base=0, pattern=[[0, 2], [-1, P]], channel_multiplier=1)
            nc.gpsimd.affine_select(out=cmp_mask[:, :, :], in_=cmp_mask[:, :, :], compare_op=ALU.is_ge, fill=NEG,
                                    base=-31, pattern=[[P, TT], [-16, CMP_M]], channel_multiplier=1).then_inc(consts, 1)

            for L in range(LAYERS):
                if L:
                    pool.wait_ge(gates_ready, 3 * L)
                    pool.wait_ge(merged, 4 * L)
                    pool.wait_ge(h_ffn, 1)
                pool.dma_start(w1, cmp_w1[L, 0].rearrange("(c p) n -> p c n", p=P)).then_inc(w1_landed, 16)
                for half in range(2):
                    pool.dma_start(w2k[:, :, HD * half:HD * half + HD], cmp_w2[L, 0].rearrange("(c p) n -> p c n", p=P)).then_inc(w2_landed, 16)
                pool.dma_start(w2v[:, :, :], cmp_w2[L, 1].rearrange("(c p) n -> p c n", p=P)).then_inc(w2_landed, 16)
                pool.dma_start(sgu_g[:, :], sgu_norm_g[L].partition_broadcast(P)).then_inc(sgug_landed, 16)
                pool.dma_start(sgu_raw, sgu_w[L].rearrange("g t s -> t g s")).then_inc(sguw_landed, 16)
                pool.wait_ge(roped, L + 1)
                pool.wait_ge(hnT_done, 8 * L + 4)
                for t in range(TT):
                    kv = tok[:, t, 512:896].rearrange("p (k c) -> p k c", k=6)
                    nc.gpsimd.tensor_copy(dup[:, t, 0:2, :].rearrange("p k (a c) -> p k a c", a=2), bc(kv[:, 0:2, :], 2, 2))
                    last = nc.gpsimd.tensor_copy(dup[:, t, 2:4, :].rearrange("p k (a c) -> p k a c", a=2), bc(kv[:, 2:5:2, :], 2, 2))
                last.then_inc(dup_ready, 1)
                pool.wait_ge(sguT_ready, L + 1)
                nc.gpsimd.affine_select(out=sgu_T[:, :, :], in_=sgu_T[:, :, :], compare_op=ALU.is_ge, fill=0.0, base=0,
                                        pattern=[[0, 4], [1, P]], channel_multiplier=-1).then_inc(sguT_cut, 1)
                for buffer, written, cut in ((att[:, :, :], sp_ready, sp_cut), (sc, aT_exp, aT_ready)):
                    if cut is aT_ready:
                        pool.wait_ge(ck_done, 2 * L + 1)
                        pool.dma_start(w1, cmp_w1[L, 1].rearrange("(c p) n -> p c n", p=P)).then_inc(w1_landed, 16)
                    pool.wait_ge(written, L + 1)
                    for diagonal in (buffer[:, :, 0:P], buffer[:, :, 2 * P:3 * P]):
                        last = nc.gpsimd.affine_select(out=diagonal, in_=diagonal, compare_op=ALU.is_gt, fill=0.0, base=0,
                                                       pattern=[[0, HEADS], [1, P]], channel_multiplier=-1)
                    last.then_inc(cut, 1)
                load_gain(2 * L + 1, norm2_g[L])
                if L == 0:
                    load_gain(2, norm1_g[1])
            load_gain(4, final_norm_g)

            pool.wait_ge(h_mixed, 2)
            pool.dma_start(rw[:, :, :], router_w[0].rearrange("(k p) e -> p k e", p=P)).then_inc(rw_landed, 16)
            nc.gpsimd.memset(pick[:, EXPERTS, :, :], 0.0)
            nc.gpsimd.iota(slot_no[:, :], pattern=[[1, P]], base=0, channel_multiplier=0,
                           allow_small_or_imprecise_dtypes=True).then_inc(consts, 1)

            def copies(half):
                pool.wait_ge(spread_ready, 4 * half + 4)
                if half:
                    pool.wait_ge(scatter_done, EXPERTS)
                nc.gpsimd.tensor_copy(spread_e[:, :], spread[:, 0, :]).then_inc(spread_e_ready, 1)
                with pool.Fori(1, EXPERTS) as i:
                    pool.wait_ge(scatter_done, i + EXPERTS * half)
                    nc.gpsimd.tensor_copy(spread_e[:, :], spread[:, i, :]).then_inc(spread_e_ready, 1)
            copies(0)
            pool.wait_ge(most_ready, 1)
            with pool.If(pool.value_load(most_i[0:1, 0:1], min_val=0, max_val=T) > CAPACITY):
                copies(1)

        @block.scalar
        def _(act):
            at = [0]

            def split_to(u):
                while at[0] <= u:
                    split_hi(act, at[0], **odd_shape(at[0]))
                    at[0] += 1

            def norm_roots():
                for t in range(TT):
                    norms[0] += 1
                    act.wait_ge(sq_ready, norms[0])
                    nc.scalar.activation(rstd[:, t:t + 1], ssq[:, t:t + 1], ACT.Sqrt, bias=eps[:, 0:1], scale=1.0 / D).then_inc(rt_ready, 1)
            norms = [0]

            def transposed(n, banks, dst, ready):
                for b in range(4):
                    act.wait_ge(hnT_done, 4 * n + b + 1)
                    nc.scalar.activation(dst[:, 2 * b:2 * b + 2, :].rearrange("p a t -> p (a t)"), psum[:, banks + b, :], ACT.Copy).then_inc(ready, 1)

            act.wait_ge(consts, 1)
            for L in range(LAYERS):
                base = MIX1_U * L
                norm_roots()
                split_to(base + 1)
                transposed(2 * L, 0, xT_hi, xT_hi_ready)
                if L == 0:
                    act.wait_ge(small_T, 1)
                    nc.scalar.activation(posT[:, :], psum[:, 7, 0:64], ACT.Copy)
                    nc.scalar.activation(biasT[:, :, :].rearrange("p l g -> p (l g)"), psum[:, 7, 64:72], ACT.Copy).then_inc(small_T_ready, 1)
                split_to(base + 2)
                act.wait_ge(unit_used, base + 1)
                nc.scalar.activation(sbT[:, 0:2, :].rearrange("p a t -> p (a t)"), psum[:, 4, :], ACT.Copy)
                split_to(base + 3)
                act.wait_ge(unit_used, base + 2)
                nc.scalar.activation(sbT[:, 2:4, :].rearrange("p a t -> p (a t)"), psum[:, 5, :], ACT.Copy).then_inc(sbT_ready, 1)
                split_to(base + 5)
                act.wait_ge(unit_used, base + 4)
                nc.scalar.activation(tok[:, :, 0:512], psum[:, 6:8, :], ACT.Copy).then_inc(tokA_ready, 1)
                split_to(base + 7)
                act.wait_ge(unit_used, base + 6)
                nc.scalar.activation(tok[:, :, 512:PT_N], psum[:, 0:2, 0:CKV_N], ACT.Copy).then_inc(tokB_ready, 1)
                split_to(base + 9)
                act.wait_ge(unit_used, base + 8)
                nc.scalar.activation(uv[:, :, :], psum[:, 2:4, :], ACT.Gelu_apprx_tanh).then_inc(uv_ready, 1)
                act.wait_ge(zs_ready, L + 1)
                for n, (src, func, scale, bias) in enumerate(((sc, ACT.Abs, 1.0, 0.0), (att[:, :, :], ACT.Exp, -1.0, 0.0), (att[:, :, :], ACT.Ln, 1.0, 1.0))):
                    nc.scalar.activation(att[:, :, :], src, func, scale=scale, bias=bias).then_inc(soft_ready, 1)
                    act.wait_ge(soft_ready, 3 * L + n + 1)

                def gate_copy(n):
                    act.wait_ge(unit_used, base + 8 + n + 1)
                    c = 2 * ((n + 8) % 12)
                    nc.scalar.activation(gates[:, c:c + 2, :].rearrange("p a t -> p (a t)"), psum[:, n % 2, :], ACT.Copy).then_inc(gate_copied, 1)

                gate_copy(0)
                act.wait_ge(kTp_done, L + 1)
                nc.scalar.activation(kT[:, :, :].rearrange("p (b k) t -> p b (k t)", b=2), psum[:, 2:4, :], ACT.Copy).then_inc(kT_ready, 1)
                split_to(base + 10)
                gate_copy(1)
                act.wait_ge(qTp_done, L + 1)
                nc.scalar.activation(qT[:, :, :].rearrange("p a t -> p (a t)"), psum[:, 2, :], ACT.Copy).then_inc(qT_ready, 1)
                act.wait_ge(sguTp_done, L + 1)
                if L:
                    act.wait_ge(mix_done, L)
                nc.scalar.activation(sgu_T[:, :, :].rearrange("p a t -> p (a t)"), psum[:, 3, :], ACT.Copy).then_inc(sguT_ready, 1)
                split_to(base + 11)
                act.wait_ge(vsq_ready, L + 1)
                nc.scalar.activation(small[:, 2:4], small[:, 0:2], ACT.Sqrt, bias=eps[:, 0:1], scale=1.0 / T).then_inc(vrt_ready, 1)
                gate_copy(2)
                split_to(base + 12)
                act.wait_ge(ck_done, 2 * L + 1)
                nc.scalar.activation(hid_c[:, 0, :], psum[0:CMP_M, 2, 0:256], ACT.Gelu_apprx_tanh).then_inc(hc_ready, 1)
                gate_copy(3)
                split_to(base + 13)
                act.wait_ge(hcT_done, 2 * L + 1)
                nc.scalar.activation(hid_cT[:, 0, :, :], psum[:, 3, 0:32].rearrange("p (a m) -> p a m", a=2)[:, :, 0:CMP_M], ACT.Copy).then_inc(hcT_ready, 1)
                act.wait_ge(ck_done, 2 * L + 2)
                nc.scalar.activation(hid_c[:, 1, :], psum[0:CMP_M, 3, 0:256], ACT.Gelu_apprx_tanh).then_inc(hc_ready, 1)
                nc.scalar.activation(small[:, 16:40].rearrange("p (t g) -> p t g", t=TT), tok[:, :, 896:908], ACT.Sigmoid).then_inc(gsig, 1)
                act.wait_ge(kc_done, 2 * L + 1)
                nc.scalar.activation(kcT[:, :], psum[:, 2, 0:CMP_M], ACT.Copy).then_inc(kc_ready, 1)
                act.wait_ge(arg_ready, L + 1)
                nc.scalar.activation(sc, sc, ACT.Exp).then_inc(aT_exp, 1)
                act.wait_ge(hcT_done, 2 * L + 2)
                nc.scalar.activation(hid_cT[:, 1, :, :], psum[:, 3, 0:32].rearrange("p (a m) -> p a m", a=2)[:, :, 0:CMP_M], ACT.Copy).then_inc(hcT_ready, 1)
                gate_copy(4)
                split_to(base + 14)
                act.wait_ge(kc_done, 2 * L + 2)
                nc.scalar.activation(vc[:, :], psum[0:CMP_M, 2, 0:HD], ACT.Copy).then_inc(kc_ready, 1)
                act.wait_ge(yb_done, L + 1)
                nc.scalar.activation(y_hi[:, 1, :, :].rearrange("p a t -> p (a t)"), psum[:, 2, :], ACT.Copy).then_inc(yb_hi, 1)
                gate_copy(5)
                split_to(base + 15)
                act.wait_ge(yaT_done, L + 1)
                nc.scalar.activation(y_hi[:, 0, :, :].rearrange("p a t -> p (a t)"), psum[:, 3, :], ACT.Copy).then_inc(ya_hi, 1)

                def exps(n):
                    act.wait_ge(sm_ready, 3 * L + n + 1)
                    for hh in range(HEADS):
                        nc.scalar.activation(sc[:, hh, 0:P], sc[:, hh, 0:P], ACT.Exp, scale=SCALE,
                                             bias=small[:, 48 + hh:49 + hh], accum_out=small[:, 56 + hh:57 + hh])
                        last = nc.scalar.activation(sc[:, hh, P:3 * P], sc[:, hh, P:3 * P], ACT.Exp, scale=SCALE,
                                                    bias=small[:, 52 + hh:53 + hh], accum_out=small[:, 60 + hh:61 + hh])
                    last.then_inc(p_exp, 1)

                def pT_copy(n):
                    act.wait_ge(pT_done, 3 * L + n + 1)
                    nc.scalar.activation(att[:, :, :], psum[:, 4:8, 0:384], ACT.Copy).then_inc(pT_ready, 1)
                exps(0)
                gate_copy(6)
                split_to(base + 16)
                pT_copy(0)
                gate_copy(7)
                split_to(base + 17)
                exps(1)
                gate_copy(8)
                split_to(base + 18)
                pT_copy(1)
                gate_copy(9)
                split_to(base + 19)
                act.wait_ge(sm_ready, 3 * L + 3)
                nc.scalar.activation(pc[:, :, :, :, :], pc[:, :, :, :, :], ACT.Exp, scale=SCALE).then_inc(p_exp, 1)
                gate_copy(10)
                split_to(base + 20)
                act.wait_ge(pT_done, 3 * L + 3)
                nc.scalar.activation(att[0:CMP_M, :, 0:T].rearrange("p (b a) t -> p b a t", b=2),
                                     psum[0:CMP_M, 6:8, :].rearrange("p b (a t) -> p b a t", a=2), ACT.Copy).then_inc(pT_ready, 1)
                gate_copy(11)
                split_to(base + 21)
                act.wait_ge(yc_ready, L + 1)
                nc.scalar.activation(y_hi[:, 2, :, :], ysum, ACT.Copy).then_inc(yc_hi, 1)
                act.wait_ge(gate_copied, 12 * L + 12)
                for n in range(3):
                    nc.scalar.activation(gates[:, 8 * n:8 * n + 8, :], gates[:, 8 * n:8 * n + 8, :], ACT.Sigmoid).then_inc(gates_ready, 1)
                split_to(base + 24)
                for b in range(4):
                    act.wait_ge(merged, 4 * L + b + 1)
                    nc.scalar.activation(xT_hi[:, 2 * b:2 * b + 2, :].rearrange("p a t -> p (a t)"),
                                         gates[:, 2 * b:2 * b + 2, :].rearrange("p a t -> p (a t)"), ACT.Copy).then_inc(mg_hi, 1)
                split_to(base + MIX_UNITS - 1)
                norm_roots()
                if L == 0:
                    split_to(FFN_U + 1)
                    transposed(1, 4, xT_hi, xT_hi_ready)

                    def group(g, i, par, w=512):
                        act.wait_ge(unit_used, i * 6 + (FFN_U + max(3 * g, 1)))
                        if not (isinstance(i, int) and g == 0):
                            act.wait_ge(f_hid_ready, i * 2 + g)
                        nc.scalar.activation(f_silu[:, 0:w], psum[:, 4 + 2 * par, 0:w], ACT.Silu).then_inc(f_silu_ready, 1)

                    def high(g, i, par):
                        act.wait_ge(f_hid_ready, i * 2 + (g + 1))
                        nc.scalar.activation(f_hi[:, par, :, :].rearrange("p a t -> p (a t)"), f_hid[:, :], ACT.Copy).then_inc(f_hi_ready, 1)
                    split_to(FFN_U + 3)
                    group(0, 0, 0)
                    high(0, 0, 0)
                    assert at[0] == FFN_U + 4
                    with act.Fori(0, 4) as i:
                        for b in range(2):
                            u = FFN_U + 4 + 3 * b
                            split_hi(act, u, i, 6)
                            group(1 + b, i, (1 + b) % 2)
                            split_hi(act, u + 1, i, 6)
                            high(1 + b, i, (1 + b) % 2)
                            split_hi(act, u + 2, i, 6)
                    at[0] = FFN_U + 28
                    for g in (9, 10):
                        split_to(FFN_U + 3 * g + 1)
                        group(g, 0, g % 2)
                        split_to(FFN_U + 3 * g + 2)
                        high(g, 0, g % 2)
                        split_to(FFN_U + 3 * g + 3)

            transposed(3, 4, xTf, xTf_ready)
            act.wait_ge(dv_ready, 1)
            nc.scalar.activation(ex[:, :, 0], ex[:, :, 1], ACT.Exp).then_inc(ex_ready, 1)

            def expert_pass(half, start):
                e0, s0 = EXPERTS * half, EXPERTS * STEPS * half
                def gathered(i, c):
                    act.wait_ge(gather_done, i + (c + 1))
                    nc.scalar.activation(sel_hi[:, :, :].rearrange("p (b k) s -> p b (k s)", b=2), psum[:, 5:7, :], ACT.Copy).then_inc(sel_hi_ready, 1)

                def values(i, c, u):
                    act.wait_ge(unit_used, i * PER_EXPERT + (u + 1))
                    if not (isinstance(i, int) and c + i == 0):
                        act.wait_ge(scatter_done, i + c)
                    nc.scalar.activation(y_e[:, :].rearrange("p (b n) -> p b n", b=2), psum[:, 3:5, :], ACT.Copy).then_inc(y_e_ready, 1)

                def expert(i, first):
                    base = start - 2
                    for j in range(STEPS):
                        n = s0 + j
                        for u in range(base + 6 * j + 2, base + 6 * j + 6):
                            split_hi(act, u, i, PER_EXPERT)
                        act.wait_ge(unit_used, i * PER_EXPERT + (base + 6 * j + 2 + 2 * (first and j == 0)))
                        if not (first and n == 0):
                            act.wait_ge(e_hid_ready, i * STEPS + n)
                        nc.scalar.activation(e_silu[:, :], psum[:, 0, :], ACT.Silu).then_inc(e_silu_ready, 1)
                        if j == STEPS - 1:
                            gathered(i, e0 + half + 1)
                        if j == 0 and not first:
                            values(i, e0 - 1, base + 5)
                        for u in (base + 6 * j + 6, base + 6 * j + 7):
                            split_hi(act, u, i, PER_EXPERT)
                        act.wait_ge(e_T, i * STEPS + (n + 1))
                        nc.scalar.activation(eT_hi[:, :, :].rearrange("p a s -> p (a s)"), psum[:, 2, :], ACT.Copy).then_inc(eT_hi_ready, 1)
                gathered(0, e0 + half)
                for b in range(4):
                    act.wait_ge(spreadT_done, 4 * half + b + 1)
                    nc.scalar.activation(spread[:, 2 * b:2 * b + 2, :].rearrange("p e t -> p (e t)"), psum[:, 1 + b, :], ACT.Copy).then_inc(spread_ready, 1)
                expert(0, True)
                with act.Fori(1, EXPERTS) as i:
                    expert(i, False)
                values(0, e0 + EXPERTS - 1, start + MOE_UNITS - 1)
            expert_pass(0, MOE_U)
            act.wait_ge(most_ready, 1)
            with act.If(act.value_load(most_i[0:1, 0:1], min_val=0, max_val=T) > CAPACITY):
                expert_pass(1, MOE_U + MOE_UNITS)
            norm_roots()

        @block.vector
        def _(dve):
            at = [0]
            done = [0]
            norms = [0]

            def step(ins):
                done[0] += 1
                ins.then_inc(dve_step, 1)
                dve.wait_ge(dve_step, done[0])

            def split_to(u):
                while at[0] <= u:
                    split_lo(dve, at[0], **odd_shape(at[0]))
                    at[0] += 1
            V = nc.vector

            def norm(n, ready):
                for t in range(TT):
                    V.tensor_tensor_reduce(out=hn[:, t, :], in0=h[:, t, :], in1=h[:, t, :], scale=1.0, scalar=0.0,
                                           op0=ALU.mult, op1=ALU.add, accum_out=ssq[:, t:t + 1]).then_inc(sq_ready, 1)
                dve.wait_ge(gain_landed, 16 * (n + 1))
                for t in range(TT):
                    dve.wait_ge(rt_ready, 2 * n + t + 1)
                    step(V.reciprocal(rstd[:, t:t + 1], rstd[:, t:t + 1]))
                    V.scalar_tensor_tensor(out=hn[:, t, :], in0=h[:, t, :], scalar=rstd[:, t:t + 1], in1=gain[:, :],
                                           op0=ALU.mult, op1=ALU.mult).then_inc(ready, 1)

            def transposed_lo(n, banks):
                for b in range(4):
                    dve.wait_ge(xT_hi_ready, 4 * n + b + 1)
                    o = (slice(None), slice(2 * b, 2 * b + 2), slice(None))
                    V.tensor_tensor(xT_lo[o].rearrange("p a t -> p (a t)"), psum[:, banks + b, :],
                                    xT_hi[o].rearrange("p a t -> p (a t)").bitcast(F32), ALU.subtract).then_inc(xT_ready, 1)

            dve.wait_ge(x_landed, 16)
            for L in range(LAYERS):
                base = MIX1_U * L
                n0 = 2 * L
                norm(n0, hn_ready)
                split_to(base + 1)
                for b in range(4):
                    dve.wait_ge(xT_hi_ready, 8 * L + b + 1)
                    o = (slice(None), slice(2 * b, 2 * b + 2), slice(None))
                    V.tensor_tensor(xT_lo[o].rearrange("p a t -> p (a t)"), psum[:, b, :],
                                    xT_hi[o].rearrange("p a t -> p (a t)").bitcast(F32), ALU.subtract).then_inc(xT_ready, 1)
                split_to(base + 7)
                if L == 0:
                    dve.wait_ge(rope_landed, 16)
                    dve.wait_ge(small_T_ready, 1)
                dve.wait_ge(tokB_ready, L + 1)
                dve.wait_ge(tokA_ready, L + 1)
                tmp = small[:, 64:64 + 2 * 2 * 4 * 8 * 1].rearrange("p (a t h c) -> p a t h c", a=2, t=TT, h=4)
                for k, (c0, stride, count) in enumerate(((256, HD, 4), (512, 2 * HD, 3))):
                    grp = tok[:, :, c0:c0 + stride * count].rearrange("p t (h c) -> p t h c", h=count)
                    x1, x2 = grp[:, :, :, 0:8], grp[:, :, :, 8:16]
                    cos, nsin, sin = (bc(rope_sb[:, :, a, :], 2, count) for a in range(3))
                    b1, b2 = tmp[:, 0, :, 0:count, :], tmp[:, 1, :, 0:count, :]
                    V.tensor_tensor(b1, x2, nsin, ALU.mult)
                    step(V.tensor_tensor(b2, x1, sin, ALU.mult))
                    V.tensor_tensor(x1, x1, cos, ALU.mult)
                    step(V.tensor_tensor(x2, x2, cos, ALU.mult))
                    V.tensor_tensor(x1, x1, b1, ALU.add)
                    last = V.tensor_tensor(x2, x2, b2, ALU.add)
                    if k:
                        last.then_inc(roped, 1)
                    else:
                        step(last)
                split_to(base + 8)
                dve.wait_ge(uv_ready, L + 1)
                for t in range(TT):
                    last = V.tensor_tensor_reduce(out=att[:, t, 0:256],
                                                  in0=uv[:, t, 256:512], in1=uv[:, t, 256:512], scale=1.0, scalar=0.0,
                                                  op0=ALU.mult, op1=ALU.add, accum_out=small[:, t:t + 1])
                last.then_inc(vsq_ready, 1)
                split_to(base + 9)
                dve.wait_ge(z_done, L + 1)
                dve.wait_ge(kTp_done, L + 1)
                V.tensor_scalar(sc, psum[:, 4:8, 0:384], SCALE, None, ALU.mult).then_inc(zs_ready, 1)
                dve.wait_ge(soft_ready, 3 * L + 3)
                step(V.scalar_tensor_tensor(out=att[:, :, :], in0=sc, scalar=0.0, in1=att[:, :, :], op0=ALU.max, op1=ALU.add))
                V.tensor_tensor(sc, sc, att[:, :, :], ALU.subtract).then_inc(sp_ready, 1)
                dve.wait_ge(kT_ready, L + 1)
                for half in range(2):
                    rows = slice(HD * half, HD * half + HD)
                    for c8 in range(2):
                        src = kT[rows, 0:2, :].rearrange("p v (m l) -> p v l m", l=16)[:, :, half:16:2, c8:c8 + CMP_M]
                        pos = posT[rows, 32 * L:32 * L + 32].rearrange("p (v c) -> p v c", v=2)[:, :, 8 * c8:8 * c8 + 8]
                        last = V.tensor_tensor(blk[rows, :, 8 * c8:8 * c8 + 8, :], src, bc(pos, 3, CMP_M), ALU.add)
                last.then_inc(blk_ready, 1)
                split_to(base + 11)
                dve.wait_ge(vrt_ready, L + 1)
                step(V.reciprocal(small[:, 4:6], small[:, 2:4]))
                dve.wait_ge(sgug_landed, 16 * (L + 1))
                for t in range(TT):
                    last = V.scalar_tensor_tensor(out=uv[:, t, 256:512], in0=uv[:, t, 256:512], scalar=small[:, 4 + t:5 + t],
                                                  in1=sgu_g[:, :], op0=ALU.mult, op1=ALU.mult)
                last.then_inc(vn_ready, 1)
                dve.wait_ge(btw_done, L + 1)
                V.tensor_tensor(sc, sc, psum[:, 4:8, 0:384], ALU.subtract).then_inc(arg_ready, 1)
                split_to(base + 12)
                dve.wait_ge(mix_done, L + 1)
                mix = psum[:, 3, :].rearrange("p (t g d) -> p t g d", t=TT, g=4)
                for t in range(TT):
                    last = V.tensor_tensor(uv[:, t, 256:512].rearrange("p (g d) -> p g d", g=4), mix[:, t, :, :],
                                           bc(biasT[:, L, :], 2, HD), ALU.add)
                step(last)
                V.tensor_tensor(uv[:, :, 0:256], uv[:, :, 0:256], uv[:, :, 256:512], ALU.mult).then_inc(ya_ready, 1)
                split_to(base + 14)
                dve.wait_ge(yb_hi, L + 1)
                V.tensor_tensor(y_lo[:, 1, :, :].rearrange("p a t -> p (a t)"), psum[:, 2, :],
                                y_hi[:, 1, :, :].rearrange("p a t -> p (a t)").bitcast(F32), ALU.subtract).then_inc(y_ready, 1)

                def scores(n):
                    dve.wait_ge(s_done, 3 * L + n + 1)
                    step(V.tensor_tensor(sc, psum[:, 4:8, 0:384], bc(causal[:, :, :].rearrange("p b k -> p (b k)"), 1, HEADS), ALU.add))
                    V.tensor_reduce(small[:, 40:44], sc[:, :, 0:P], AX_X, ALU.max)
                    step(V.tensor_reduce(small[:, 44:48], sc[:, :, P:3 * P], AX_X, ALU.max))
                    V.tensor_scalar(small[:, 48:56], small[:, 40:48], -SCALE, None, ALU.mult).then_inc(sm_ready, 1)

                def weights(n, branch):
                    dve.wait_ge(p_exp, 3 * L + n + 1)
                    dve.wait_ge(gsig, L + 1)
                    step(V.reciprocal(small[:, 128:136], small[:, 56:64]))
                    g = small[:, 16:40].rearrange("p (t h b) -> p t h b", t=TT, b=3)[:, :, :, branch]
                    step(V.tensor_tensor(small[:, 136:144].rearrange("p (t h) -> p t h", t=TT), small[:, 128:136].rearrange("p (t h) -> p t h", t=TT), g, ALU.mult))
                    V.tensor_tensor(sc[:, :, 0:P], sc[:, :, 0:P], bc(small[:, 136:140], 2, P), ALU.mult)
                    V.tensor_tensor(sc[:, :, P:3 * P], sc[:, :, P:3 * P], bc(small[:, 140:144], 2, 2 * P), ALU.mult).then_inc(p_ready, 1)
                scores(0)
                split_to(base + 15)
                dve.wait_ge(ya_hi, L + 1)
                V.tensor_tensor(y_lo[:, 0, :, :].rearrange("p a t -> p (a t)"), psum[:, 3, :],
                                y_hi[:, 0, :, :].rearrange("p a t -> p (a t)").bitcast(F32), ALU.subtract).then_inc(y_ready, 1)
                weights(0, 1)
                split_to(base + 16)
                dve.wait_ge(av_done, 3 * L + 1)
                V.tensor_copy(ysum.rearrange("p a t -> p (a t)"), psum[:, 2, :]).then_inc(av_added, 1)
                scores(1)
                split_to(base + 17)
                weights(1, 2)
                split_to(base + 18)
                dve.wait_ge(av_done, 3 * L + 2)
                dve.wait_ge(av_added, 2 * L + 1)
                V.tensor_tensor(ysum.rearrange("p a t -> p (a t)"), ysum.rearrange("p a t -> p (a t)"), psum[:, 2, :], ALU.add).then_inc(av_added, 1)
                dve.wait_ge(s_done, 3 * L + 3)
                pcf = pc[:, :, :, :, :].rearrange("p a t j m -> p (a t j) m")
                for half in range(2):
                    last = V.tensor_tensor(pc[:, half, :, :, :], psum[:, 4 + half, 0:64].rearrange("p (t j m) -> p t j m", t=TT, j=2)[:, :, :, 0:CMP_M],
                                           bc(cmp_mask[:, :, :], 2, 2), ALU.add)
                step(last)
                step(V.tensor_reduce(small[:, 144:152], pcf, AX_X, ALU.max))
                step(V.tensor_scalar(small[:, 152:160], small[:, 144:152], NEG / 10, None, ALU.max))
                V.tensor_tensor(pcf, pcf, bc(small[:, 152:160], 2, CMP_M), ALU.subtract).then_inc(sm_ready, 1)
                dve.wait_ge(p_exp, 3 * L + 3)
                step(V.tensor_reduce(small[:, 160:168], pcf, AX_X, ALU.add))
                step(V.tensor_scalar(small[:, 168:176], small[:, 160:168], 1e-30, None, ALU.max))
                step(V.reciprocal(small[:, 176:184], small[:, 168:176]))
                for half in range(2):
                    g = small[:, 16:40].rearrange("p (t j a b) -> p t j a b", t=TT, j=2, b=3)[:, :, :, half, 0]
                    last = V.tensor_tensor(small[:, 184 + 4 * half:188 + 4 * half].rearrange("p (t j) -> p t j", t=TT),
                                           small[:, 176 + 4 * half:180 + 4 * half].rearrange("p (t j) -> p t j", t=TT), g, ALU.mult)
                step(last)
                V.tensor_tensor(pcf, pcf, bc(small[:, 184:192], 2, CMP_M), ALU.mult).then_inc(p_ready, 1)
                split_to(base + 20)
                dve.wait_ge(av_done, 3 * L + 3)
                dve.wait_ge(av_added, 2 * L + 2)
                V.tensor_tensor(ysum.rearrange("p a t -> p (a t)"), ysum.rearrange("p a t -> p (a t)"), psum[:, 2, :], ALU.add).then_inc(yc_ready, 1)
                split_to(base + 21)
                dve.wait_ge(yc_hi, L + 1)
                V.tensor_tensor(y_lo[:, 2, :, :], ysum, y_hi[:, 2, :, :].bitcast(F32), ALU.subtract).then_inc(y_ready, 1)
                split_to(base + 22)
                for n in range(3):
                    dve.wait_ge(gates_ready, 3 * L + n + 1)
                    for b in range(4):
                        if b < 3:
                            dve.wait_ge(br_done, 9 * L + 3 * n + b + 1)
                        else:
                            dve.wait_ge(unit_used, base + 21 + n)
                        g = gates[:, 8 * n + 2 * b:8 * n + 2 * b + 2, :].rearrange("p a t -> p (a t)")
                        m = gates[:, 2 * b:2 * b + 2, :].rearrange("p a t -> p (a t)")
                        last = V.tensor_tensor(g, g, psum[:, (4 if n != 1 else 0) + b, :], ALU.mult)
                        if n < 2 and b == 3:
                            last.then_inc(br_used, 1)
                            dve.wait_ge(br_used, 2 * L + n + 1)
                        else:
                            step(last)
                        if n:
                            last = V.tensor_tensor(m, m, g, ALU.add)
                            if n == 2:
                                last.then_inc(merged, 1)
                    if n < 2:
                        split_to(base + 23 + n)
                for b in range(4):
                    dve.wait_ge(mg_hi, 4 * L + b + 1)
                    o = (slice(None), slice(2 * b, 2 * b + 2), slice(None))
                    V.tensor_tensor(xT_lo[o].rearrange("p a t -> p (a t)"), gates[o].rearrange("p a t -> p (a t)"),
                                    xT_hi[o].rearrange("p a t -> p (a t)").bitcast(F32), ALU.subtract).then_inc(mg_ready, 1)
                split_to(base + MIX_UNITS - 1)
                dve.wait_ge(unit_used, base + MIX_UNITS)
                for t in range(TT):
                    last = V.tensor_tensor(h[:, t, :].rearrange("p (b n) -> p b n", b=2), h[:, t, :].rearrange("p (b n) -> p b n", b=2),
                                           psum[:, 2 * t:2 * t + 2, :], ALU.add)
                last.then_inc(h_mixed, 1)
                dve.wait_ge(h_mixed, L + 1)
                norm(n0 + 1, hn_ready)
                if L == 0:
                    split_to(FFN_U + 1)
                    for b in range(4):
                        dve.wait_ge(xT_hi_ready, 4 + b + 1)
                        o = (slice(None), slice(2 * b, 2 * b + 2), slice(None))
                        V.tensor_tensor(xT_lo[o].rearrange("p a t -> p (a t)"), psum[:, 4 + b, :],
                                        xT_hi[o].rearrange("p a t -> p (a t)").bitcast(F32), ALU.subtract).then_inc(xT_ready, 1)

                    def group(g, i, par, w=512):
                        if not (isinstance(i, int) and g == 0):
                            dve.wait_ge(f_lo_ready, i * 2 + g)
                        dve.wait_ge(f_silu_ready, i * 2 + (g + 1))
                        dve.wait_ge(unit_used, i * 6 + (FFN_U + max(3 * g + 1, 2)))
                        V.tensor_tensor(f_hid[:, 0:w], f_silu[:, 0:w], psum[:, 5 + 2 * par, 0:w], ALU.mult).then_inc(f_hid_ready, 1)

                    def low(g, i, par):
                        dve.wait_ge(f_hi_ready, i * 2 + (g + 1))
                        V.tensor_tensor(f_lo[:, par, :, :].rearrange("p a t -> p (a t)"), f_hid[:, :],
                                        f_hi[:, par, :, :].rearrange("p a t -> p (a t)").bitcast(F32), ALU.subtract).then_inc(f_lo_ready, 1)
                    split_to(FFN_U + 3)
                    group(0, 0, 0)
                    low(0, 0, 0)
                    with dve.Fori(0, 4) as i:
                        for b in range(2):
                            u = FFN_U + 4 + 3 * b
                            split_lo(dve, u, i, 6)
                            group(1 + b, i, (1 + b) % 2)
                            split_lo(dve, u + 1, i, 6)
                            low(1 + b, i, (1 + b) % 2)
                            split_lo(dve, u + 2, i, 6)
                    at[0] = FFN_U + 28
                    for g in (9, 10):
                        split_to(FFN_U + 3 * g + 1)
                        group(g, 0, g % 2)
                        split_to(FFN_U + 3 * g + 2)
                        low(g, 0, g % 2)
                        split_to(FFN_U + 3 * g + 3)
                    dve.wait_ge(unit_used, MIX1_U)
                    for t in range(TT):
                        last = V.tensor_tensor(h[:, t, :].rearrange("p (b n) -> p b n", b=2), h[:, t, :].rearrange("p (b n) -> p b n", b=2),
                                               psum[:, 2 * t:2 * t + 2, :], ALU.add)
                    last.then_inc(h_ffn, 1)
                    dve.wait_ge(h_ffn, 1)

            dve.wait_ge(lg_done, 1)
            dve.wait_ge(consts, 2)
            step(V.tensor_copy(lg[:, :, :], psum[:, 0, 0:16].rearrange("p (t e) -> p t e", t=TT)))
            for t in range(TT):
                step(V.max(top_v[:, t, :], lg[:, t, :]))
                step(V.max_index(top_i[:, t, :], top_v[:, t, :], lg[:, t, :]))
            V.tensor_copy(top_f[:, :, :], top_i[:, :, 0:2])
            V.tensor_tensor(ex[:, :, 1], top_v[:, :, 1], top_v[:, :, 0], ALU.subtract).then_inc(dv_ready, 1)
            dve.wait_ge(ex_ready, 1)
            step(V.tensor_scalar(ex[:, :, 1], ex[:, :, 0], 1.0, None, ALU.add))
            step(V.reciprocal(ex[:, :, 1], ex[:, :, 1]))
            step(V.tensor_tensor(ex[:, :, 0], ex[:, :, 0], ex[:, :, 1], ALU.mult))
            for n in range(2):
                step(V.tensor_tensor(hit[:, n, :, :], bc(slot_no[:, 0:EXPERTS], 1, TT), bc(top_f[:, :, n], 2, EXPERTS), ALU.is_equal))
            V.tensor_tensor(chosen[:, :, :], hit[:, 0, :, :], hit[:, 1, :, :], ALU.add).then_inc(chosen_ready, 1)
            dve.wait_ge(chosen_ready, 1)
            for n in range(2):
                step(V.tensor_tensor(hit[:, n, :, :], hit[:, n, :, :], bc(ex[:, :, 1 - n], 2, EXPERTS), ALU.mult))
            step(V.tensor_tensor(gate[:, :, :], hit[:, 0, :, :], hit[:, 1, :, :], ALU.add))
            dve.wait_ge(pos_done, 1)
            step(V.scalar_tensor_tensor(out=place[:, :, :], in0=psum[:, 1, 0:16].rearrange("p (t e) -> p t e", t=TT), scalar=1.0,
                                        in1=chosen[:, :, :], op0=ALU.add, op1=ALU.mult))
            step(V.tensor_scalar(place[:, :, :], place[:, :, :], -1.0, None, ALU.add))
            step(V.tensor_reduce(most[:, :], psum[:, 1, 16:24], AX_X, ALU.max))
            V.tensor_copy(most_i[:, :], most[:, :]).then_inc(most_ready, 1)

            def expert_pass(half, start, step):
                e0, s0 = EXPERTS * half, EXPERTS * STEPS * half
                if half:
                    dve.wait_ge(h_added, EXPERTS)
                    step(V.tensor_scalar(place[:, :, :], place[:, :, :], float(-CAPACITY), None, ALU.add))
                for c in range(TT):
                    last = V.tensor_tensor(pick[:, 0:EXPERTS, c, :], bc(slot_no[:, :], 1, EXPERTS), bc(place[:, c, :], 2, P), ALU.is_equal)
                last.then_inc(pick_ready, 1)
                dve.wait_ge(pick_ready, half + 1)
                for c in range(TT):
                    last = V.tensor_tensor(gated[:, :, c, :], pick[:, 0:EXPERTS, c, :], bc(gate[:, c, :], 2, P), ALU.mult)
                last.then_inc(gated_ready, 1)

                def gathered(i, c):
                    dve.wait_ge(sel_hi_ready, i + (c + 1))
                    V.tensor_tensor(sel_lo[:, :, :].rearrange("p (b k) s -> p b (k s)", b=2), psum[:, 5:7, :],
                                    sel_hi[:, :, :].rearrange("p (b k) s -> p b (k s)", b=2).bitcast(F32), ALU.subtract).then_inc(sel_ready, 1)

                def add(i, c):
                    dve.wait_ge(scatter_done, i + (c + 1))
                    for t in range(TT):
                        for n in range(2):
                            bank = (5, 6, 7, 2)[2 * t + n]
                            hh = h[:, t, 512 * n:512 * n + 512]
                            last = V.tensor_tensor(hh, hh, psum[:, bank, :], ALU.add)
                    last.then_inc(h_added, 1)

                def expert(i, first):
                    base = start - 2
                    for j in range(STEPS):
                        n = s0 + j
                        for u in range(base + 6 * j + 2, base + 6 * j + 6):
                            split_lo(dve, u, i, PER_EXPERT)
                        dve.wait_ge(e_silu_ready, i * STEPS + (n + 1))
                        dve.wait_ge(unit_used, i * PER_EXPERT + (base + 6 * j + 4 + 2 * (first and j == 0)))
                        if not (first and n == 0):
                            dve.wait_ge(e_T, i * STEPS + n)
                        V.tensor_tensor(e_hid[:, :], e_silu[:, :], psum[:, 1, :], ALU.mult).then_inc(e_hid_ready, 1)
                        if j == STEPS - 1:
                            gathered(i, e0 + half + 1)
                        if j == 1 and not first:
                            add(i, e0 - 1)
                        for u in (base + 6 * j + 6, base + 6 * j + 7):
                            split_lo(dve, u, i, PER_EXPERT)
                        dve.wait_ge(eT_hi_ready, i * STEPS + (n + 1))
                        V.tensor_tensor(eT_lo[:, :, :].rearrange("p a s -> p (a s)"), psum[:, 2, :],
                                        eT_hi[:, :, :].rearrange("p a s -> p (a s)").bitcast(F32), ALU.subtract).then_inc(eT_ready, 1)
                gathered(0, e0 + half)
                expert(0, True)
                with dve.Fori(1, EXPERTS) as i:
                    expert(i, False)
                add(0, e0 + EXPERTS - 1)
                dve.wait_ge(h_added, EXPERTS * (half + 1))
            expert_pass(0, MOE_U, step)
            with dve.If(dve.value_load(most_i[0:1, 0:1], min_val=0, max_val=T) > CAPACITY):
                rest = [0]

                def rest_of(ins):
                    rest[0] += 1
                    ins.then_inc(rest_step, 1)
                    dve.wait_ge(rest_step, rest[0])
                expert_pass(1, MOE_U + MOE_UNITS, rest_of)
            norm(4, out_ready)

        @block.tensor
        def _(pe):
            M = nc.tensor

            def transpose_hn(n, banks):
                for t in range(TT):
                    pe.wait_ge(hn_ready, 2 * n + t + 1)
                    for k in range(KC):
                        c = (k % 2) * T + t * P
                        last = M.transpose(psum[:, banks + k // 2, c:c + P], hn[:, t, k * P:(k + 1) * P], ident[:, :])
                        if t == TT - 1 and k % 2:
                            last.then_inc(hnT_done, 1)

            def rows(L, u, chunks, bank, n=UNIT, used=True):
                w = unit(pe, u, KC, n=n)
                for c in range(chunks):
                    width = min(P, n // KC - c * P)
                    for k in range(KC):
                        last = mm3(psum[0:width, bank, c * T:(c + 1) * T], [a[:, k, c * P:c * P + width] for a in w],
                                   [a[:, k, :] for a in xT], k == 0, k == KC - 1)
                return last

            def tokens(u, width, bank):
                for half in range(2):
                    w = unit(pe, u + half, 4, n=4 * width)
                    for t in range(TT):
                        for k in range(4):
                            kk = 4 * half + k
                            last = mm3(psum[:, bank + t, 0:width], [a[:, kk, t * P:(t + 1) * P] for a in xT],
                                       [a[:, k, :] for a in w], kk == 0, kk == KC - 1)
                    last.then_inc(unit_used, 1)

            pe.wait_ge(consts, 1)
            for L in range(LAYERS):
                base = MIX1_U * L
                transpose_hn(2 * L, 0)
                if L == 0:
                    pe.wait_ge(posb_landed, 32)
                    M.transpose(psum[:, 7, 0:64], pos_b, ident[0:64, 0:64])
                    M.transpose(psum[:, 7, 64:72], sb_b, ident[0:8, 0:8]).then_inc(small_T, 1)
                pe.wait_ge(xT_ready, 8 * L + 4)
                for n in range(2):
                    rows(L, base + n, 2, 4 + n).then_inc(unit_used, 1)
                if L == 0:
                    pe.wait_ge(small_T_ready, 1)
                for n, (width, bank) in enumerate(((512, 6), (CKV_N, 0), (512, 2))):
                    tokens(base + 2 + 2 * n, width, bank)

                def gate_unit(n):
                    if n >= 2:
                        pe.wait_ge(gate_copied, 12 * L + n - 1)
                    else:
                        pe.wait_ge(tokB_ready, L + 1)
                    rows(L, base + 8 + n, 2, n % 2).then_inc(unit_used, 1)

                pe.wait_ge(sbT_ready, L + 1)
                pe.wait_ge(tokA_ready, L + 1)
                for hh in range(HEADS):
                    r, j = slice(HD * (hh % 2), HD * (hh % 2) + HD), hh // 2
                    M.matmul(psum[:, 4 + hh, 0:T], sbT[r, 2 + j, 0:P], sbT[r, j, :], start=True, stop=True)
                    last = M.matmul(psum[:, 4 + hh, T:T + P], sbT[r, 2 + j, P:T], sbT[r, j, P:T], start=True, stop=True)
                last.then_inc(z_done, 1)
                gate_unit(0)
                pe.wait_ge(dup_ready, L + 1)
                pe.wait_ge(uv_ready, L + 1)
                for k in range(4):
                    for t in range(TT):
                        c = (k % 2) * T + t * P
                        last = M.transpose(psum[:, 2 + k // 2, c:c + P], dup[:, t, k, :], ident[:, :])
                last.then_inc(kTp_done, 1)
                gate_unit(1)
                pe.wait_ge(kT_ready, L + 1)
                for a in range(2):
                    for t in range(TT):
                        last = M.transpose(psum[:, 2, a * T + t * P:a * T + (t + 1) * P], tok[:, t, 256 + a * P:256 + (a + 1) * P], ident[:, :])
                last.then_inc(qTp_done, 1)
                pe.wait_ge(sguw_landed, 16 * (L + 1))
                for g in range(4):
                    last = M.transpose(psum[:, 3, g * P:(g + 1) * P], sgu_raw[:, g, :], ident[:, :])
                last.then_inc(sguTp_done, 1)
                gate_unit(2)
                pe.wait_ge(blk_ready, L + 1)
                pe.wait_ge(qT_ready, L + 1)
                pe.wait_ge(w1_landed, 32 * L + 16)
                for c in range(CMP_C):
                    last = M.matmul(psum[0:CMP_M, 2, 0:256], blk[:, 0, c, :], w1[:, c, :], start=c == 0, stop=c == CMP_C - 1)
                last.then_inc(ck_done, 1)
                pe.wait_ge(sp_cut, L + 1)
                for hh in range(HEADS):
                    M.matmul(psum[:, 4 + hh, 0:T], later[:, :], att[:, hh, 0:T], start=True, stop=False)
                    M.matmul(psum[:, 4 + hh, P:T], ones[:, :], att[:, hh, T:T + P], start=False, stop=True)
                    last = M.matmul(psum[:, 4 + hh, T:T + P], later[:, :], att[:, hh, T:T + P], start=True, stop=True)
                last.then_inc(btw_done, 1)
                pe.wait_ge(vn_ready, L + 1)
                pe.wait_ge(sguT_cut, L + 1)
                for t in range(TT):
                    for g in range(4):
                        c = t * 256 + g * HD
                        last = M.matmul(psum[:, 3, c:c + HD], sgu_T[:, g, :], uv[:, t, 256 + g * HD:256 + (g + 1) * HD], start=True, stop=True)
                last.then_inc(mix_done, 1)
                gate_unit(3)
                pe.wait_ge(ya_ready, L + 1)

                def hidden_T(v):
                    pe.wait_ge(hc_ready, 2 * L + v + 1)
                    for a in range(2):
                        last = M.transpose(psum[:, 3, 16 * a:16 * a + CMP_M], hid_c[:, v, a * P:(a + 1) * P], ident[0:CMP_M, 0:CMP_M])
                    last.then_inc(hcT_done, 1)
                hidden_T(0)
                pe.wait_ge(hcT_ready, 2 * L + 1)
                pe.wait_ge(w2_landed, 48 * (L + 1))
                for a in range(2):
                    last = M.matmul(psum[:, 2, 0:CMP_M], w2k[:, a, :], hid_cT[:, 0, a, :], start=a == 0, stop=a == 1)
                last.then_inc(kc_done, 1)
                pe.wait_ge(w1_landed, 32 * L + 32)
                for c in range(CMP_C):
                    last = M.matmul(psum[0:CMP_M, 3, 0:256], blk[:, 1, c, :], w1[:, c, :], start=c == 0, stop=c == CMP_C - 1)
                last.then_inc(ck_done, 1)
                gate_unit(4)
                hidden_T(1)
                pe.wait_ge(hcT_ready, 2 * L + 2)
                pe.wait_ge(kc_ready, 2 * L + 1)
                for a in range(2):
                    last = M.matmul(psum[0:CMP_M, 2, 0:HD], hid_cT[:, 1, a, :], w2v[:, a, :], start=a == 0, stop=a == 1)
                last.then_inc(kc_done, 1)
                pe.wait_ge(aT_ready, L + 1)
                pe.wait_ge(kc_ready, 2 * L + 2)
                for hh in range(HEADS):
                    r, j = slice(HD * (hh % 2), HD * (hh % 2) + HD), hh // 2
                    M.matmul(psum[r, 2, j * T:(j + 1) * T], tok[:, 0, hh * HD:(hh + 1) * HD], sc[:, hh, 0:T], start=True, stop=False)
                    last = M.matmul(psum[r, 2, j * T + P:(j + 1) * T], tok[:, 1, hh * HD:(hh + 1) * HD], sc[:, hh, T:T + P], start=False, stop=True)
                last.then_inc(yb_done, 1)

                def scores(n):
                    if n == 0:
                        pe.wait_ge(arg_ready, L + 1)
                    else:
                        pe.wait_ge(pT_ready, 3 * L + 1)
                    for hh in range(HEADS):
                        r, j = slice(HD * (hh % 2), HD * (hh % 2) + HD), hh // 2
                        M.matmul(psum[:, 4 + hh, 0:P], qT[r, j, 0:P], kT[r, 2 + n, 0:P], start=True, stop=True)
                        last = M.matmul(psum[:, 4 + hh, P:3 * P], qT[r, j, P:T], kT[r, 2 + n, :], start=True, stop=True)
                    last.then_inc(s_done, 1)

                def weights_T(n):
                    pe.wait_ge(p_ready, 3 * L + n + 1)
                    for hh in range(HEADS):
                        for b in range(3):
                            last = M.transpose(psum[:, 4 + hh, b * P:(b + 1) * P], sc[:, hh, b * P:(b + 1) * P], ident[:, :])
                    last.then_inc(pT_done, 1)

                def outputs(n, c0):
                    pe.wait_ge(pT_ready, 3 * L + n + 1)
                    if n == 0:
                        pe.wait_ge(y_ready, 3 * L + 1)
                    else:
                        pe.wait_ge(av_added, 2 * L + n)
                    for hh in range(HEADS):
                        r, j = slice(HD * (hh % 2), HD * (hh % 2) + HD), hh // 2
                        M.matmul(psum[r, 2, j * T:(j + 1) * T], tok[:, 0, c0:c0 + HD], att[:, hh, 0:T], start=True, stop=False)
                        last = M.matmul(psum[r, 2, j * T + P:(j + 1) * T], tok[:, 1, c0:c0 + HD], att[:, hh, T:T + P], start=False, stop=True)
                    last.then_inc(av_done, 1)
                scores(0)
                gate_unit(5)
                for a in range(2):
                    for t in range(TT):
                        last = M.transpose(psum[:, 3, a * T + t * P:a * T + (t + 1) * P], uv[:, t, a * P:(a + 1) * P], ident[:, :])
                last.then_inc(yaT_done, 1)
                gate_unit(6)
                weights_T(0)
                gate_unit(7)
                outputs(0, 512 + 3 * HD)
                scores(1)
                gate_unit(8)
                weights_T(1)
                gate_unit(9)
                outputs(1, 512 + 5 * HD)
                for half in range(2):
                    r = slice(HD * half, HD * half + HD)
                    for t in range(TT):
                        for j in range(2):
                            c = 16 * (2 * t + j)
                            last = M.matmul(psum[:, 4 + half, c:c + CMP_M], qT[r, j, t * P:(t + 1) * P], kcT[r, :], start=True, stop=True)
                last.then_inc(s_done, 1)
                gate_unit(10)
                pe.wait_ge(p_ready, 3 * L + 3)
                for half in range(2):
                    for t in range(TT):
                        for j in range(2):
                            hh = 2 * j + half
                            c = (hh % 2) * T + t * P
                            last = M.transpose(psum[0:CMP_M, 6 + hh // 2, c:c + P], pc[:, half, t, j, :], ident[:, :])
                last.then_inc(pT_done, 1)
                gate_unit(11)
                pe.wait_ge(pT_ready, 3 * L + 3)
                pe.wait_ge(av_added, 2 * L + 2)
                for hh in range(HEADS):
                    r, j = slice(HD * (hh % 2), HD * (hh % 2) + HD), hh // 2
                    last = M.matmul(psum[r, 2, j * T:(j + 1) * T], vc[:, :], att[0:CMP_M, hh, 0:T], start=True, stop=True)
                last.then_inc(av_done, 1)
                pe.wait_ge(y_ready, 3 * L + 2)
                for n in range(3):
                    if n == 1:
                        pe.wait_ge(yc_ready, L + 1)
                        pe.wait_ge(gate_copied, 12 * L + 12)
                    if n == 2:
                        pe.wait_ge(y_ready, 3 * L + 3)
                        pe.wait_ge(br_used, 2 * L + 1)
                    w = unit(pe, base + 20 + n, 2)
                    for dc in range(KC):
                        for k in range(2):
                            last = mm3(psum[:, (4 if n != 1 else 0) + dc // 2, (dc % 2) * T:(dc % 2 + 1) * T],
                                       [a[:, k, dc * P:(dc + 1) * P] for a in w], [y_hi[:, n, k, :], y_lo[:, n, k, :]], k == 0, k == 1)
                        if dc % 2 and dc < KC - 1:
                            last.then_inc(br_done, 1)
                    last.then_inc(unit_used, 1)
                pe.wait_ge(br_used, 2 * L + 2)
                for n in range(4):
                    pe.wait_ge(mg_ready, 4 * L + n + 1)
                    w = unit(pe, base + 23 + n, 2)
                    for k in range(2):
                        kk = 2 * n + k
                        for t in range(TT):
                            for b in range(2):
                                last = mm3(psum[:, 2 * t + b, :], [a[:, kk, t * P:(t + 1) * P] for a in xT],
                                           [a[:, k, b * 512:(b + 1) * 512] for a in w], kk == 0, kk == KC - 1)
                    last.then_inc(unit_used, 1)
                transpose_hn(2 * L + 1, 4)
                if L == 0:
                    pe.wait_ge(xT_ready, 8)

                    def gate_up(g, i, par, u, every, n=UNIT):
                        if not (isinstance(i, int) and g < 2):
                            pe.wait_ge(f_hid_ready, i * 2 + (g - 1))
                        for k2, bank in enumerate((4 + 2 * par, 5 + 2 * par)):
                            w = unit(pe, u + k2, KC, i, every, n=n)
                            for c in range(2):
                                width = min(P, n // KC - c * P)
                                for k in range(KC):
                                    last = mm3(psum[0:width, bank, c * T:(c + 1) * T], [a[:, k, c * P:c * P + width] for a in w],
                                               [a[:, k, :] for a in xT], k == 0, k == KC - 1)
                            last.then_inc(unit_used, 1)

                    def down(g, i, par, u, every, first=False):
                        pe.wait_ge(f_lo_ready, i * 2 + (g + 1))
                        w = unit(pe, u, 2, i, every)
                        for c in range(2):
                            for t in range(TT):
                                for b in range(2):
                                    last = mm3(psum[:, 2 * t + b, :], [f[:, par, c, t * P:(t + 1) * P] for f in (f_hi, f_lo)],
                                               [a[:, c, b * 512:(b + 1) * 512] for a in w], first and c == 0, False)
                        last.then_inc(unit_used, 1)
                    gate_up(0, 0, 0, FFN_U, 6)
                    gate_up(1, 0, 1, FFN_U + 2, 6)
                    down(0, 0, 0, FFN_U + 4, 6, True)
                    gate_up(2, 0, 0, FFN_U + 5, 6)
                    down(1, 0, 1, FFN_U + 7, 6)
                    with pe.Fori(1, 4) as i:
                        for b in range(2):
                            gate_up(1 + b, i, (1 + b) % 2, FFN_U + 2 + 3 * b, 6)
                            down(b, i, b % 2, FFN_U + 4 + 3 * b, 6)
                    gate_up(9, 0, 1, FFN_U + 26, 6)
                    down(8, 0, 0, FFN_U + 28, 6)
                    gate_up(10, 0, 0, FFN_U + 29, 6, n=KC * FT)
                    down(9, 0, 1, FFN_U + 31, 6)
                    pe.wait_ge(f_lo_ready, 11)
                    for c, parts in enumerate((P, FT - P)):
                        w = unit(pe, FFN_U + 32 + c, 1, parts=parts, n=D)
                        for t in range(TT):
                            for b in range(2):
                                last = mm3(psum[:, 2 * t + b, :], [f[0:parts, 0, c, t * P:(t + 1) * P] for f in (f_hi, f_lo)],
                                           [a[:, 0, b * 512:(b + 1) * 512] for a in w], False, c == 1)
                        last.then_inc(unit_used, 1)

            pe.wait_ge(xTf_ready, 4)
            pe.wait_ge(rw_landed, 16)
            for t in range(TT):
                for k in range(KC):
                    last = M.matmul(psum[:, 0, t * 8:t * 8 + 8], xTf[:, k, t * P:(t + 1) * P], rw[:, k, :], start=k == 0, stop=k == KC - 1)
            last.then_inc(lg_done, 1)
            pe.wait_ge(chosen_ready, 1)
            M.matmul(psum[:, 1, 0:8], before[:, :], chosen[:, 0, :], start=True, stop=True)
            M.matmul(psum[:, 1, 8:16], before[:, :], chosen[:, 1, :], start=True, stop=False)
            M.matmul(psum[:, 1, 8:16], ones[:, :], chosen[:, 0, :], start=False, stop=True)
            M.matmul(psum[:, 1, 16:24], ones[:, :], chosen[:, 0, :], start=True, stop=False)
            M.matmul(psum[:, 1, 16:24], ones[:, :], chosen[:, 1, :], start=False, stop=True).then_inc(pos_done, 1)

            def expert_pass(half, start):
                e0, s0 = EXPERTS * half, EXPERTS * STEPS * half

                def gather(e):
                    for k in range(KC):
                        for c in range(TT):
                            last = M.matmul(psum[:, 5 + k // 4, (k % 4) * P:(k % 4 + 1) * P], hn[:, c, k * P:(k + 1) * P],
                                            pick[:, e, c, :], start=c == 0, stop=c == TT - 1)
                    last.then_inc(gather_done, 1)

                def scatter(i, c):
                    pe.wait_ge(y_e_ready, i + (c + 1))
                    pe.wait_ge(spread_e_ready, i + (c + 1))
                    for t in range(TT):
                        for n in range(2):
                            last = M.matmul(psum[:, (5, 6, 7, 2)[2 * t + n], :], spread_e[:, t * P:(t + 1) * P],
                                            y_e[:, 512 * n:512 * n + 512], start=True, stop=True)
                    last.then_inc(scatter_done, 1)

                def down(i, j, u, n):
                    pe.wait_ge(eT_ready, i * STEPS + (n + 1))
                    for hf in range(2):
                        w = unit(pe, u + hf, 2, i, PER_EXPERT)
                        for f in range(2):
                            ff = 2 * hf + f
                            for b in range(2):
                                last = mm3(psum[:, 3 + b, :], [a[:, ff, :] for a in (eT_hi, eT_lo)],
                                           [a[:, f, 512 * b:512 * b + 512] for a in w], j == 0 and ff == 0, j == STEPS - 1 and ff == 3)
                        last.then_inc(unit_used, 1)

                def expert(i, first):
                    base = start - 2
                    for j in range(STEPS):
                        n = s0 + j
                        shift = 2 if first and j == 0 else 0
                        if j == 0:
                            pe.wait_ge(sel_ready, i + (e0 + half + 1))
                        for k2, freed in enumerate((e_silu_ready, e_hid_ready)):
                            if not (first and n == 0):
                                pe.wait_ge(freed, i * STEPS + n)
                            if first and j == 0 and k2:
                                pe.wait_ge(spread_ready, 4 * half + 4)
                            for hf in range(2):
                                w = unit(pe, base + 6 * j + shift + 2 * k2 + hf, 4, i, PER_EXPERT)
                                for k in range(4):
                                    kk = 4 * hf + k
                                    last = mm3(psum[:, k2, :], [a[:, kk, :] for a in (sel_hi, sel_lo)],
                                               [a[:, k, :] for a in w], kk == 0, kk == KC - 1)
                                last.then_inc(unit_used, 1)
                        if j == 0 and not first:
                            down(i, STEPS - 1, base + 4, s0 - 1)
                        if j == 1 and not first:
                            scatter(i, e0 - 1)
                            pe.wait_ge(h_added, i + e0)
                        if j == STEPS - 1:
                            gather(i + 1)
                        if j:
                            down(i, j - 1, base + 6 * j + 4, n - 1)
                        pe.wait_ge(e_hid_ready, i * STEPS + (n + 1))
                        for f in range(4):
                            last = M.transpose(psum[:, 2, f * P:(f + 1) * P], e_hid[:, f * P:(f + 1) * P], ident[:, :])
                        last.then_inc(e_T, 1)

                pe.wait_ge(pick_ready, half + 1)
                gather(0)
                pe.wait_ge(gated_ready, half + 1)
                for e in range(EXPERTS):
                    for c in range(TT):
                        last = M.transpose(psum[:, 1 + e // 2, (e % 2) * T + c * P:(e % 2) * T + (c + 1) * P], gated[:, e, c, :], ident[:, :])
                    if e % 2:
                        last.then_inc(spreadT_done, 1)
                expert(0, True)
                with pe.Fori(1, EXPERTS) as i:
                    expert(i, False)
                down(0, STEPS - 1, start + MOE_UNITS - 2, s0 + EXPERTS * STEPS - 1)
                scatter(0, e0 + EXPERTS - 1)
            expert_pass(0, MOE_U)
            pe.wait_ge(most_ready, 1)
            with pe.If(pe.value_load(most_i[0:1, 0:1], min_val=0, max_val=T) > CAPACITY):
                expert_pass(1, MOE_U + MOE_UNITS)


_INS = ["x", "norm1_g", "w_in", "sgu_norm_g", "sgu_w", "sgu_b", "cmp_pos", "cmp_w1", "cmp_w2", "w_branch", "w_out",
        "norm2_g", "ffn_w_gate", "ffn_w_up", "ffn_w_down", "router_w", "moe_w_gate", "moe_w_up", "moe_w_down",
        "final_norm_g"]


def kernel(**inputs):
    import numpy as _np
    import concourse.bacc as _bacc
    from concourse.bass_utils import run_bass_kernel_spmd as _run

    nc = _bacc.Bacc("TRN2", target_bir_lowering=False, num_devices=1)
    arrays, args = {}, []
    freq = (500000.0 ** (-_np.arange(0, 16, 2, dtype=_np.float32) / 16)).astype(_np.float32)
    ang = _np.arange(T, dtype=_np.float32)[:, None] * freq[None, :]
    table = _np.concatenate([_np.cos(ang), -_np.sin(ang), _np.sin(ang)], axis=1).astype(_np.float32)
    for name in _INS + ["rope"]:
        a = _np.ascontiguousarray(inputs[name]) if name != "rope" else table
        arrays[f"in_{name}"] = a
        args.append(nc.dram_tensor(f"in_{name}", a.shape, mybir.dt.from_np(a.dtype), kind="ExternalInput").ap())
    args.append(nc.dram_tensor("out_0", (1, T, D), F32, kind="ExternalOutput").ap())
    hybrid_trunk(nc, *args)
    r = _run(nc, [arrays], core_ids=[0])
    return r.results[0]["out_0"]
```

```python
from contextlib import ExitStack

import concourse.bass as bass
from concourse import mybir

F32 = mybir.dt.float32
F32R = mybir.dt.float32r
I32 = mybir.dt.int32
U32 = mybir.dt.uint32
ALU = mybir.AluOpType
ACT = mybir.ActivationFunctionType
AX_X = mybir.AxisListType.X

P = 128
LAYERS = 2
D = 1024
T = 256
TT = T // P
KC = D // P
HD = 64
HEADS = 4
A0, SB0, TOK0, CKV0, GATE0 = 0, 512, 1024, 1536, 1932
CKV_N = GATE0 - CKV0
PT_N = 512 + CKV_N
CMP_M = (T - 32) // 16 + 1
SPREAD_BANKS = (2, 3, 4, 7)
CMP_C = 32 * HD // P
D_FF = 2752
FG = 256
FFN_FULL = D_FF // FG
FT = D_FF - FFN_FULL * FG
EXPERTS = 8
D_E = 3584
STEPS = D_E // 512
CAPACITY = P
EPS = 1e-6
NEG = -1e30
SCALE = HD ** -0.5

UNIT = 2048
RAW = 6
SPLIT = 3
MIX_UNITS = 27
FFN_UNITS = 3 * FFN_FULL + 4
PER_EXPERT = 6 * STEPS
FFN_U = MIX_UNITS
MIX1_U = FFN_U + FFN_UNITS
MOE_U = MIX1_U + MIX_UNITS
MOE_UNITS = EXPERTS * PER_EXPERT


def bc(ap, axis, n):
    a = ap.unsqueeze(axis)
    shape = list(a.shape)
    shape[axis] = n
    return a.broadcast_to(shape)


def hybrid_trunk(nc, x, norm1_g, w_in, sgu_norm_g, sgu_w, sgu_b, cmp_pos, cmp_w1, cmp_w2, w_branch, w_out,
                 norm2_g, ffn_w_gate, ffn_w_up, ffn_w_down, router_w, moe_w_gate, moe_w_up, moe_w_down,
                 final_norm_g, rope, out):
    ctx = ExitStack()
    with ctx:
        def sb(name, shape, dt=F32):
            return ctx.enter_context(nc.sbuf_tensor(name, shape, dt))

        def sem(name):
            return ctx.enter_context(nc.semaphore(name))

        raw = sb("raw", [P, RAW, UNIT])
        w_hi = sb("w_hi", [P, SPLIT, UNIT], F32R)
        w_lo = sb("w_lo", [P, SPLIT, UNIT], F32R)
        h = sb("h", [P, TT, D])
        hn = sb("hn", [P, TT, D])
        xT_hi = sb("xT_hi", [P, KC, T], F32R)
        xT_lo = sb("xT_lo", [P, KC, T], F32R)
        gain = sb("gain", [P, D])
        ident = sb("ident", [P, P])
        ones = sb("ones", [P, P])
        later = sb("later", [P, P])
        before = sb("before", [P, P])
        causal = sb("causal", [P, 3, P])
        cmp_mask = sb("cmp_mask", [P, TT, CMP_M])
        rope_sb = sb("rope_sb", [P, TT, 3, 8])
        eps = sb("eps", [P, 1])
        unused = sb("unused", [P, 8])
        ssq = sb("ssq", [P, TT])
        rstd = sb("rstd", [P, TT])
        psum = ctx.enter_context(nc.psum_tensor("psum", [P, 8, 512], F32))

        with ExitStack() as own:
            def mb(name, shape, dt=F32):
                return own.enter_context(nc.sbuf_tensor(name, shape, dt))
            gates = mb("gates", [P, 24, T])
            tok = mb("tok", [P, TT, PT_N])
            sbT = mb("sbT", [P, 4, T])
            uv = mb("uv", [P, TT, 512])
            qT = mb("qT", [P, 2, T])
            kT = mb("kT", [P, 4, T])
            att = mb("att", [P, HEADS, 384])
            y_hi = mb("y_hi", [P, 3, 2, T], F32R)
            y_lo = mb("y_lo", [P, 3, 2, T], F32R)
            sgu_T = mb("sgu_T", [P, 4, P])
            sgu_g = mb("sgu_g", [P, T])
            small = mb("small", [P, 256])
            posT = mb("posT", [P, 64])
            biasT = mb("biasT", [P, LAYERS, 4])
            w2k = mb("w2k", [P, 2, P])
            w2v = mb("w2v", [P, 2, HD])
            hid_cT = mb("hid_cT", [P, 2, 2, CMP_M])
            kcT = mb("kcT", [P, CMP_M])
            vc = mb("vc", [CMP_M, HD])
            blk = mb("blk", [P, 2, CMP_C, CMP_M])
            pc = mb("pc", [P, 2, TT, 2, CMP_M])
        with ExitStack() as own:
            def mb(name, shape, dt=F32):
                return own.enter_context(nc.sbuf_tensor(name, shape, dt))
            f_silu = mb("f_silu", [P, 512])
            f_hid = mb("f_hid", [P, 512])
            f_hi = mb("f_hi", [P, 2, 2, T], F32R)
            f_lo = mb("f_lo", [P, 2, 2, T], F32R)
        with ExitStack() as own:
            def mb(name, shape, dt=F32):
                return own.enter_context(nc.sbuf_tensor(name, shape, dt))
            pick = mb("pick", [P, EXPERTS + 1, TT, P])
            spread = mb("spread", [P, EXPERTS, T])
            spread_e = mb("spread_e", [P, T])
            sel_hi = mb("sel_hi", [P, KC, P], F32R)
            sel_lo = mb("sel_lo", [P, KC, P], F32R)
            y_e = mb("y_e", [P, D])
            e_silu = mb("e_silu", [P, 512])
            e_hid = mb("e_hid", [P, 512])
            eT_hi = mb("eT_hi", [P, 4, P], F32R)
            eT_lo = mb("eT_lo", [P, 4, P], F32R)
            xTf = mb("xTf", [P, KC, T])
            gated = mb("gated", [P, EXPERTS, TT, P])
            slot_no = mb("slot_no", [P, P])
            rw = mb("rw", [P, KC, EXPERTS])
            lg = mb("lg", [P, TT, EXPERTS])
            top_v = mb("top_v", [P, TT, 8])
            top_i = mb("top_i", [P, TT, 8], U32)
            top_f = mb("top_f", [P, TT, 2])
            ex = mb("ex", [P, TT, 2])
            hit = mb("hit", [P, 2, TT, EXPERTS])
            gate = mb("gate", [P, TT, EXPERTS])
            chosen = mb("chosen", [P, TT, EXPERTS])
            place = mb("place", [P, TT, EXPERTS])
            most = mb("most", [P, 1])
            most_i = mb("most_i", [P, 1], I32)

        scr = hn[:, :, :].rearrange("p t d -> p (t d)")
        dup = gates[:, 2:6, :].rearrange("p a (k c) -> p (a k) c", k=2).rearrange("p (t k) c -> p t k c", t=TT)
        sc = scr[:, 0:1536].rearrange("p (h c) -> p h c", h=HEADS)
        hid_c = scr[0:CMP_M, 1536:2048].rearrange("p (v c) -> p v c", v=2)
        w1 = gates[:, 8:24, :]
        sgu_raw = gates[:, 6:8, :].rearrange("p a (g s) -> p (a g) s", g=2)
        pos_b, sb_b = gates[0:64, 4, 0:P], gates[0:8, 5, 0:P]
        ysum = kT[:, 0:2, :]

        landed = [sem(f"landed{n}") for n in range(RAW)]
        hi_ready, lo_ready, unit_used = sem("hi_ready"), sem("lo_ready"), sem("unit_used")
        x_landed = [sem(f"x_landed{t}") for t in range(TT)]
        rope_landed, rw_landed = sem("rope_landed"), sem("rw_landed")
        posb_landed, w2_landed, sguw_landed, sgug_landed = sem("posb_landed"), sem("w2_landed"), sem("sguw_landed"), sem("sgug_landed")
        w1_landed = sem("w1_landed")
        gain_landed = sem("gain_landed")
        consts, pool_step, eps_ready = sem("consts"), sem("pool_step"), sem("eps_ready")
        sq_ready, rt_ready, hn_ready, hnT_done, xT_hi_ready, xT_ready = (
            sem("sq_ready"), sem("rt_ready"), sem("hn_ready"), sem("hnT_done"), sem("xT_hi_ready"), sem("xT_ready"))
        dve_step, act_sum, tile0_done = sem("dve_step"), sem("act_sum"), sem("tile0_done")
        sbT_ready, tokA_ready, tokB_ready, uv_ready = sem("sbT_ready"), sem("tokA_ready"), sem("tokB_ready"), sem("uv_ready")
        roped, dup_ready, kTp_done, kT_ready = sem("roped"), sem("dup_ready"), sem("kTp_done"), sem("kT_ready")
        qTp_done, qT_ready, sguTp_done, sguT_ready, sguT_cut = sem("qTp_done"), sem("qT_ready"), sem("sguTp_done"), sem("sguT_ready"), sem("sguT_cut")
        gate_copied, gates_ready = sem("gate_copied"), sem("gates_ready")
        z_done, zs_ready, soft_ready, sp_ready, sp_cut = sem("z_done"), sem("zs_ready"), sem("soft_ready"), sem("sp_ready"), sem("sp_cut")
        btw_done, arg_ready, aT_exp, aT_ready, yb_done, yb_hi = sem("btw_done"), sem("arg_ready"), sem("aT_exp"), sem("aT_ready"), sem("yb_done"), sem("yb_hi")
        small_T, small_T_ready = sem("small_T"), sem("small_T_ready")
        blk_ready, ck_done, hc_ready, hcT_done, hcT_ready, kc_done, kc_ready = (
            sem("blk_ready"), sem("ck_done"), sem("hc_ready"), sem("hcT_done"), sem("hcT_ready"), sem("kc_done"), sem("kc_ready"))
        vsq_ready, vrt_ready, vn_ready, mix_done, ya_ready, yaT_done, ya_hi = (
            sem("vsq_ready"), sem("vrt_ready"), sem("vn_ready"), sem("mix_done"), sem("ya_ready"), sem("yaT_done"), sem("ya_hi"))
        gsig = sem("gsig")
        s_done, sm_ready, p_exp, p_ready, pT_done, pT_ready, av_done, av_added, yc_ready, yc_hi, y_ready = (
            sem("s_done"), sem("sm_ready"), sem("p_exp"), sem("p_ready"), sem("pT_done"), sem("pT_ready"),
            sem("av_done"), sem("av_added"), sem("yc_ready"), sem("yc_hi"), sem("y_ready"))
        br_done, br_used, merged, mg_hi, mg_ready, h_mixed = (
            sem("br_done"), sem("br_used"), sem("merged"), sem("mg_hi"), sem("mg_ready"), sem("h_mixed"))
        f_silu_ready, f_hid_ready, f_hi_ready, f_lo_ready, h_ffn = (
            sem("f_silu_ready"), sem("f_hid_ready"), sem("f_hi_ready"), sem("f_lo_ready"), sem("h_ffn"))
        xTf_ready, lg_done, dv_ready, ex_ready, chosen_ready, pos_done, most_ready = (
            sem("xTf_ready"), sem("lg_done"), sem("dv_ready"), sem("ex_ready"), sem("chosen_ready"), sem("pos_done"), sem("most_ready"))
        pick_ready, gated_ready, spreadT_done, spread_ready, spread_e_ready = (
            sem("pick_ready"), sem("gated_ready"), sem("spreadT_done"), sem("spread_ready"), sem("spread_e_ready"))
        gather_done, sel_hi_ready, sel_ready = sem("gather_done"), sem("sel_hi_ready"), sem("sel_ready")
        e_silu_ready, e_hid_ready, e_T, eT_hi_ready, eT_ready = (
            sem("e_silu_ready"), sem("e_hid_ready"), sem("e_T"), sem("eT_hi_ready"), sem("eT_ready"))
        y_e_ready, scatter_done, h_added, rest_step = (
            sem("y_e_ready"), sem("scatter_done"), sem("h_added"), sem("rest_step"))
        tile0_scattered = sem("tile0_scattered")
        two_merged = sem("two_merged")
        out_ready, stored = sem("out_ready"), sem("stored")

        def load_unit(sp, u, src, i=0, every=0, parts=P):
            if u >= RAW:
                sp.wait_ge(lo_ready, i * every + (u - RAW + 1))
            n = 1
            for s in src.shape[1:]:
                n *= s
            dst = raw[0:parts, u % RAW, 0:n]
            if len(src.shape) == 3:
                dst = dst.rearrange("p (a b) -> p a b", a=src.shape[1])
            sp.dma_start(dst, src).then_inc(landed[u % RAW], 16)

        def split_hi(act, u, i=0, every=0, parts=P, n=UNIT):
            act.wait_ge(landed[u % RAW], i * (every // RAW * 16) + 16 * (u // RAW + 1))
            if u >= SPLIT:
                act.wait_ge(unit_used, i * every + (u - SPLIT + 1))
            nc.scalar.activation(w_hi[0:parts, u % SPLIT, 0:n], raw[0:parts, u % RAW, 0:n], ACT.Copy).then_inc(hi_ready, 1)

        def split_lo(dve, u, i=0, every=0, parts=P, n=UNIT):
            dve.wait_ge(hi_ready, i * every + (u + 1))
            if u >= SPLIT:
                dve.wait_ge(unit_used, i * every + (u - SPLIT + 1))
            nc.vector.tensor_tensor(w_lo[0:parts, u % SPLIT, 0:n], raw[0:parts, u % RAW, 0:n],
                                    w_hi[0:parts, u % SPLIT, 0:n].bitcast(F32), ALU.subtract).then_inc(lo_ready, 1)

        def unit(pe, u, a, i=0, every=0, parts=P, n=UNIT):
            pe.wait_ge(lo_ready, i * every + (u + 1))
            return [w[0:parts, u % SPLIT, 0:n].rearrange("p (a b) -> p a b", a=a) for w in (w_hi, w_lo)]

        def mm3(o, lhs, rhs, start, stop):
            nc.tensor.matmul(o, lhs[0], rhs[0], start=start, stop=False)
            nc.tensor.matmul(o, lhs[0], rhs[1], start=False, stop=False)
            return nc.tensor.matmul(o, lhs[1], rhs[0], start=False, stop=stop)

        def odd_shape(u):
            for base in (0, MIX1_U):
                if u - base in (4, 5):
                    return {"n": 4 * CKV_N}
            if u in (FFN_U + 3 * FFN_FULL - 1, FFN_U + 3 * FFN_FULL):
                return {"n": KC * FT}
            if u == FFN_U + 3 * FFN_FULL + 2:
                return {"n": D}
            if u == FFN_U + 3 * FFN_FULL + 3:
                return {"n": D, "parts": FT - P}
            return {}

        xT = (xT_hi, xT_lo)
        block = ctx.enter_context(nc.Block())

        @block.sync
        def _(sp):
            for t in range(TT):
                sp.dma_start(h[:, t, :], x[0, t * P:(t + 1) * P, :]).then_inc(x_landed[t], 16)

            def mixer_units(L, base):
                w = w_in[L].rearrange("(k p) n -> p k n", p=P)
                for n in range(2):
                    load_unit(sp, base + n, w[:, :, SB0 + n * 256:SB0 + (n + 1) * 256])
                for n, (c, width) in enumerate(((TOK0, 512), (CKV0, CKV_N), (A0, 512))):
                    for half in range(2):
                        load_unit(sp, base + 2 + 2 * n + half, w[:, 4 * half:4 * half + 4, c:c + width])
                for n in range(12):
                    c = GATE0 + n * 256
                    load_unit(sp, base + 8 + n, w[:, :, c:c + 256])
                for n in range(3):
                    load_unit(sp, base + 20 + n, w_branch[L, n].rearrange("(k p) n -> p k n", p=P))
                for n in range(4):
                    load_unit(sp, base + 23 + n, w_out[L].rearrange("(k p) n -> p k n", p=P)[:, 2 * n:2 * n + 2, :])

            mixer_units(0, 0)
            fg, fu = (w[0].rearrange("(k p) n -> p k n", p=P) for w in (ffn_w_gate, ffn_w_up))

            def ffn_down(g):
                return ffn_w_down[0, bass.ds(g * FG, FG), :].rearrange("(k p) n -> p k n", p=P)
            load_unit(sp, FFN_U, fg[:, :, 0:FG])
            load_unit(sp, FFN_U + 1, fu[:, :, 0:FG])
            with sp.Fori(0, 4) as i:
                for b in range(2):
                    u = FFN_U + 2 + 3 * b
                    load_unit(sp, u, fg[:, :, bass.ds(i * (2 * FG) + (b + 1) * FG, FG)], i, 6)
                    load_unit(sp, u + 1, fu[:, :, bass.ds(i * (2 * FG) + (b + 1) * FG, FG)], i, 6)
                    load_unit(sp, u + 2, ffn_down(i * 2 + b), i, 6)
            u, c = FFN_U + 26, 9 * FG
            load_unit(sp, u, fg[:, :, c:c + FG])
            load_unit(sp, u + 1, fu[:, :, c:c + FG])
            load_unit(sp, u + 2, ffn_down(8))
            load_unit(sp, u + 3, fg[:, :, D_FF - FT:D_FF])
            load_unit(sp, u + 4, fu[:, :, D_FF - FT:D_FF])
            load_unit(sp, u + 5, ffn_down(9))
            load_unit(sp, u + 6, ffn_w_down[0, D_FF - FT:D_FF - FT + P, :])
            load_unit(sp, u + 7, ffn_w_down[0, D_FF - FT + P:D_FF, :], parts=FT - P)
            mixer_units(1, MIX1_U)

            def expert_units(base, i, first):
                eg, eu = (w[0, i if first else bass.ds(i, 1)].rearrange("(k p) n -> p k n" if first else "a (k p) n -> p (a k) n", p=P)
                          for w in (moe_w_gate, moe_w_up))

                def down(e, j, u, k):
                    for half in range(2):
                        r = 512 * j + 256 * half
                        src = moe_w_down[0, bass.ds(e, 1), r:r + 256, :].rearrange("a (k p) n -> p (a k) n", p=P)
                        load_unit(sp, u + half, src, k, PER_EXPERT)
                for j in range(STEPS):
                    shift = 2 if first and j == 0 else 0
                    for n, w in enumerate((eg, eu)):
                        for half in range(2):
                            load_unit(sp, base + 6 * j + shift + 2 * n + half,
                                      w[:, 4 * half:4 * half + 4, 512 * j:512 * j + 512], i, PER_EXPERT)
                    if j:
                        down(i, j - 1, base + 6 * j + 4, i)
                    elif not first:
                        down(i - 1, STEPS - 1, base + 4, i)

            def expert_stream(start):
                expert_units(start - 2, 0, True)
                with sp.Fori(1, EXPERTS) as i:
                    expert_units(start - 2, i, False)
                for half in range(2):
                    r = 512 * (STEPS - 1) + 256 * half
                    load_unit(sp, start + MOE_UNITS - 2 + half,
                              moe_w_down[0, EXPERTS - 1, r:r + 256, :].rearrange("(k p) n -> p k n", p=P))
            expert_stream(MOE_U)
            sp.wait_ge(most_ready, 1)
            with sp.If(sp.value_load(most_i[0:1, 0:1], min_val=0, max_val=T) > CAPACITY):
                expert_stream(MOE_U + MOE_UNITS)
            for t in range(TT):
                sp.wait_ge(out_ready, 2 * t + 2)
                sp.dma_start(out[0, t * P:(t + 1) * P, :], hn[:, t, :]).then_inc(stored, 16)
            sp.wait_ge(stored, 16 * TT)

        @block.gpsimd
        def _(pool):
            steps = [0]

            def step(ins):
                steps[0] += 1
                ins.then_inc(pool_step, 1)
                pool.wait_ge(pool_step, steps[0])

            def load_gain(n, vector):
                if n:
                    pool.wait_ge(hn_ready, 4 * n)
                pool.dma_start(gain[:, :], vector.partition_broadcast(P)).then_inc(gain_landed, 16)
            load_gain(0, norm1_g[0])
            nc.gpsimd.memset(eps[:, :], EPS).then_inc(eps_ready, 1)
            nc.gpsimd.memset(ident[:, :], 0.0)
            nc.gpsimd.memset(ones[:, :], 1.0)
            nc.gpsimd.memset(later[:, :], 1.0)
            nc.gpsimd.memset(before[:, :], 1.0)
            nc.gpsimd.memset(cmp_mask[:, :, :], 0.0)
            step(nc.gpsimd.memset(causal[:, :, :], 0.0))
            nc.gpsimd.affine_select(out=ident[:, :], in_=ident[:, :], compare_op=ALU.not_equal, fill=1.0, base=0,
                                    pattern=[[-1, P]], channel_multiplier=1)
            nc.gpsimd.affine_select(out=later[:, :], in_=later[:, :], compare_op=ALU.is_gt, fill=0.0, base=0,
                                    pattern=[[-1, P]], channel_multiplier=1)
            nc.gpsimd.affine_select(out=before[:, :], in_=before[:, :], compare_op=ALU.is_gt, fill=0.0, base=0,
                                    pattern=[[1, P]], channel_multiplier=-1)
            nc.gpsimd.affine_select(out=causal[:, 0:3:2, :], in_=causal[:, 0:3:2, :], compare_op=ALU.is_ge, fill=NEG,
                                    base=0, pattern=[[0, 2], [-1, P]], channel_multiplier=1)
            nc.gpsimd.affine_select(out=cmp_mask[:, :, :], in_=cmp_mask[:, :, :], compare_op=ALU.is_ge, fill=NEG,
                                    base=-31, pattern=[[P, TT], [-16, CMP_M]], channel_multiplier=1).then_inc(consts, 1)
            pool.dma_start(rope_sb[:, :, :, :], rope.rearrange("(t p) (a b) -> p t a b", p=P, a=3)).then_inc(rope_landed, 16)
            pool.dma_start(pos_b, cmp_pos.rearrange("l v (c a) d -> (l v c) (a d)", a=2)).then_inc(posb_landed, 16)
            pool.dma_start(sb_b, sgu_b.rearrange("l g t -> (l g) t")).then_inc(posb_landed, 16)

            for L in range(LAYERS):
                if L:
                    pool.wait_ge(gates_ready, 3 * L)
                    pool.wait_ge(mg_ready, 4 * L)
                    pool.wait_ge(h_ffn, 2)
                pool.dma_start(w1, cmp_w1[L, 0].rearrange("(c p) n -> p c n", p=P)).then_inc(w1_landed, 16)
                for half in range(2):
                    pool.dma_start(w2k[:, :, HD * half:HD * half + HD], cmp_w2[L, 0].rearrange("(c p) n -> p c n", p=P)).then_inc(w2_landed, 16)
                pool.dma_start(w2v[:, :, :], cmp_w2[L, 1].rearrange("(c p) n -> p c n", p=P)).then_inc(w2_landed, 16)
                pool.dma_start(sgu_g[:, :], sgu_norm_g[L].partition_broadcast(P)).then_inc(sgug_landed, 16)
                pool.dma_start(sgu_raw, sgu_w[L].rearrange("g t s -> t g s")).then_inc(sguw_landed, 16)
                pool.wait_ge(roped, L + 1)
                for t in range(TT):
                    kv = tok[:, t, 512:896].rearrange("p (k c) -> p k c", k=6)
                    nc.gpsimd.tensor_copy(dup[:, t, 0:2, :].rearrange("p k (a c) -> p k a c", a=2), bc(kv[:, 0:2, :], 2, 2))
                    last = nc.gpsimd.tensor_copy(dup[:, t, 2:4, :].rearrange("p k (a c) -> p k a c", a=2), bc(kv[:, 2:5:2, :], 2, 2))
                last.then_inc(dup_ready, 1)
                for buffer, written, cut in ((att[:, :, :], sp_ready, sp_cut), (sc, aT_exp, aT_ready)):
                    pool.wait_ge(written, L + 1)
                    for diagonal in (buffer[:, :, 0:P], buffer[:, :, 2 * P:3 * P]):
                        last = nc.gpsimd.affine_select(out=diagonal, in_=diagonal, compare_op=ALU.is_gt, fill=0.0, base=0,
                                                       pattern=[[0, HEADS], [1, P]], channel_multiplier=-1)
                    last.then_inc(cut, 1)
                    if cut is sp_cut:
                        pool.wait_ge(sguT_ready, L + 1)
                        nc.gpsimd.affine_select(out=sgu_T[:, :, :], in_=sgu_T[:, :, :], compare_op=ALU.is_ge, fill=0.0, base=0,
                                                pattern=[[0, 4], [1, P]], channel_multiplier=-1).then_inc(sguT_cut, 1)
                pool.wait_ge(ck_done, 2 * L + 1)
                pool.dma_start(w1, cmp_w1[L, 1].rearrange("(c p) n -> p c n", p=P)).then_inc(w1_landed, 16)
                load_gain(2 * L + 1, norm2_g[L])
                for n in (1, 2):
                    for b in range(4):
                        g = gates[:, 8 * n + 2 * b:8 * n + 2 * b + 2, :]
                        m = gates[:, 2 * b:2 * b + 2, :]
                        pool.wait_ge(br_used, 12 * L + 4 * n + b + 1)
                        if n == 2:
                            pool.wait_ge(two_merged, 4 * L + b + 1)
                        nc.gpsimd.tensor_tensor(m, m, g, ALU.add).then_inc(two_merged if n == 1 else merged, 1)
                if L == 0:
                    load_gain(2, norm1_g[1])
            pool.wait_ge(h_mixed, 4)
            pool.dma_start(rw[:, :, :], router_w[0].rearrange("(k p) e -> p k e", p=P)).then_inc(rw_landed, 16)
            load_gain(4, final_norm_g)
            nc.gpsimd.memset(pick[:, EXPERTS, :, :], 0.0)
            nc.gpsimd.iota(slot_no[:, :], pattern=[[1, P]], base=0, channel_multiplier=0,
                           allow_small_or_imprecise_dtypes=True).then_inc(consts, 1)

            def copies(half):
                pool.wait_ge(spread_ready, 4 * half + 4)
                if half:
                    pool.wait_ge(scatter_done, EXPERTS)
                nc.gpsimd.tensor_copy(spread_e[:, :], spread[:, 0, :]).then_inc(spread_e_ready, 1)
                with pool.Fori(1, EXPERTS) as i:
                    pool.wait_ge(scatter_done, i + EXPERTS * half)
                    nc.gpsimd.tensor_copy(spread_e[:, :], spread[:, i, :]).then_inc(spread_e_ready, 1)
            copies(0)
            pool.wait_ge(most_ready, 1)
            with pool.If(pool.value_load(most_i[0:1, 0:1], min_val=0, max_val=T) > CAPACITY):
                copies(1)

        @block.scalar
        def _(act):
            at = [0]

            def split_to(u):
                while at[0] <= u:
                    split_hi(act, at[0], **odd_shape(at[0]))
                    at[0] += 1

            def root(t):
                nc.scalar.activation(rstd[:, t:t + 1], ssq[:, t:t + 1], ACT.Sqrt, bias=eps[:, 0:1], scale=1.0 / D).then_inc(rt_ready, 1)

            loads = [0]

            def load_sqrt():
                nc.scalar.activation(unused[:, loads[0]:loads[0] + 1], eps[:, 0:1], ACT.Sqrt)
                loads[0] += 1

            def norm_roots(written, counts):
                load_sqrt()
                for t in range(TT):
                    act.wait_ge(written[t], counts[t])
                    nc.scalar.activation(hn[:, t, :], h[:, t, :], ACT.Square, accum_out=ssq[:, t:t + 1]).then_inc(act_sum, 1)
                    sums[0] += 1
                    act.wait_ge(act_sum, sums[0])
                    root(t)
            sums = [0]

            def transposed(n, bank, dst, ready):
                for b in range(4):
                    act.wait_ge(hnT_done, 4 * n + b + 1)
                    k = 4 * (b % 2)
                    nc.scalar.activation(dst[:, k:k + 4, b // 2 * P:(b // 2 + 1) * P],
                                         psum[:, bank + b, :].rearrange("p (k t) -> p k t", k=4), ACT.Copy).then_inc(ready, 1)
                    if n == 0 and b == 1:
                        split_to(0)

            act.wait_ge(eps_ready, 1)
            for L in range(LAYERS):
                base = MIX1_U * L
                if L:
                    norm_roots([h_ffn] * 2, [1, 2])
                else:
                    norm_roots(x_landed, [16] * 2)
                transposed(2 * L, 0, xT_hi, xT_hi_ready)
                split_to(base + 2)
                act.wait_ge(unit_used, base + 1)
                nc.scalar.activation(sbT[:, 0:2, :].rearrange("p a t -> p (a t)"), psum[:, 4, :], ACT.Copy)
                split_to(base + 3)
                act.wait_ge(unit_used, base + 2)
                nc.scalar.activation(sbT[:, 2:4, :].rearrange("p a t -> p (a t)"), psum[:, 5, :], ACT.Copy).then_inc(sbT_ready, 1)
                if L == 0:
                    act.wait_ge(small_T, 1)
                    nc.scalar.activation(posT[:, :], psum[:, 3, 0:64], ACT.Copy)
                    nc.scalar.activation(biasT[:, :, :].rearrange("p l g -> p (l g)"), psum[:, 3, 64:72], ACT.Copy).then_inc(small_T_ready, 1)
                split_to(base + 5)
                act.wait_ge(unit_used, base + 4)
                nc.scalar.activation(tok[:, :, 0:512], psum[:, 6:8, :], ACT.Copy).then_inc(tokA_ready, 1)
                split_to(base + 7)
                act.wait_ge(unit_used, base + 6)
                nc.scalar.activation(tok[:, :, 512:PT_N], psum[:, 0:2, 0:CKV_N], ACT.Copy).then_inc(tokB_ready, 1)
                split_to(base + 9)
                act.wait_ge(unit_used, base + 8)
                nc.scalar.activation(uv[:, :, :], psum[:, 2:4, :], ACT.Gelu_apprx_tanh).then_inc(uv_ready, 1)
                split_to(base + 10)
                act.wait_ge(zs_ready, L + 1)
                for n, (src, func, scale, bias) in enumerate(((sc, ACT.Abs, 1.0, 0.0), (att[:, :, :], ACT.Exp, -1.0, 0.0), (att[:, :, :], ACT.Ln, 1.0, 1.0))):
                    nc.scalar.activation(att[:, :, :], src, func, scale=scale, bias=bias).then_inc(soft_ready, 1)
                    act.wait_ge(soft_ready, 3 * L + n + 1)

                def gate_copy(n):
                    act.wait_ge(unit_used, base + 8 + n + 1)
                    c = 2 * n
                    nc.scalar.activation(gates[:, c:c + 2, :].rearrange("p a t -> p (a t)"), psum[:, n % 2, :], ACT.Copy).then_inc(gate_copied, 1)

                gate_copy(0)
                split_to(base + 11)
                act.wait_ge(kTp_done, L + 1)
                nc.scalar.activation(kT[:, :, :].rearrange("p (b k) t -> p b (k t)", b=2), psum[:, 2:4, :], ACT.Copy).then_inc(kT_ready, 1)
                gate_copy(1)
                act.wait_ge(vsq_ready, L + 1)
                nc.scalar.activation(small[:, 2:4], small[:, 0:2], ACT.Sqrt, bias=eps[:, 0:1], scale=1.0 / T).then_inc(vrt_ready, 1)
                split_to(base + 12)
                gate_copy(2)
                split_to(base + 13)
                act.wait_ge(qTp_done, L + 1)
                nc.scalar.activation(qT[:, :, :].rearrange("p a t -> p (a t)"), psum[:, 2, :], ACT.Copy).then_inc(qT_ready, 1)
                act.wait_ge(sguTp_done, L + 1)
                if L:
                    act.wait_ge(mix_done, L)
                nc.scalar.activation(sgu_T[:, :, :].rearrange("p a t -> p (a t)"), psum[:, 3, :], ACT.Copy).then_inc(sguT_ready, 1)
                act.wait_ge(arg_ready, L + 1)
                nc.scalar.activation(sc, sc, ACT.Exp).then_inc(aT_exp, 1)
                gate_copy(3)
                split_to(base + 14)

                def hidden(v):
                    act.wait_ge(ck_done, 2 * L + v + 1)
                    nc.scalar.activation(hid_c[:, v, :], psum[0:CMP_M, 2 + v, 0:256], ACT.Gelu_apprx_tanh).then_inc(hc_ready, 1)

                def hidden_T(v):
                    act.wait_ge(hcT_done, 2 * L + v + 1)
                    nc.scalar.activation(hid_cT[:, v, :, :], psum[:, 2 + v, 0:32].rearrange("p (a m) -> p a m", a=2)[:, :, 0:CMP_M],
                                         ACT.Copy).then_inc(hcT_ready, 1)
                hidden(0)
                split_to(base + 15)
                act.wait_ge(yb_done, L + 1)
                nc.scalar.activation(y_hi[:, 1, :, :].rearrange("p a t -> p (a t)"), psum[:, 4, :], ACT.Copy).then_inc(yb_hi, 1)
                hidden_T(0)
                split_to(base + 16)
                hidden(1)
                gate_copy(4)
                gate_copy(5)
                hidden_T(1)
                act.wait_ge(kc_done, 2 * L + 1)
                nc.scalar.activation(kcT[:, :], psum[:, 2, 64:64 + CMP_M], ACT.Copy).then_inc(kc_ready, 1)
                nc.scalar.activation(small[:, 16:40].rearrange("p (t g) -> p t g", t=TT), tok[:, :, 896:908], ACT.Sigmoid).then_inc(gsig, 1)

                def exps(n):
                    act.wait_ge(sm_ready, 3 * L + n + 1)
                    for hh in range(HEADS):
                        nc.scalar.activation(sc[:, hh, 0:P], sc[:, hh, 0:P], ACT.Exp, scale=SCALE,
                                             bias=small[:, 48 + hh:49 + hh], accum_out=small[:, 56 + hh:57 + hh])
                        last = nc.scalar.activation(sc[:, hh, P:3 * P], sc[:, hh, P:3 * P], ACT.Exp, scale=SCALE,
                                                    bias=small[:, 52 + hh:53 + hh], accum_out=small[:, 60 + hh:61 + hh])
                    last.then_inc(p_exp, 1)

                def pT_copy(n):
                    act.wait_ge(pT_done, 3 * L + n + 1)
                    nc.scalar.activation(att[:, :, :], psum[:, 4:8, 0:384], ACT.Copy).then_inc(pT_ready, 1)
                exps(0)
                gate_copy(6)
                split_to(base + 17)
                act.wait_ge(kc_done, 2 * L + 2)
                nc.scalar.activation(vc[:, :], psum[0:CMP_M, 3, 64:64 + HD], ACT.Copy).then_inc(kc_ready, 1)
                act.wait_ge(yaT_done, L + 1)
                nc.scalar.activation(y_hi[:, 0, :, :].rearrange("p a t -> p (a t)"), psum[:, 2, :], ACT.Copy).then_inc(ya_hi, 1)
                gate_copy(7)
                split_to(base + 18)
                pT_copy(0)
                gate_copy(8)
                split_to(base + 19)
                exps(1)
                gate_copy(9)
                split_to(base + 20)
                gate_copy(10)
                pT_copy(1)
                split_to(base + 21)
                gate_copy(11)
                act.wait_ge(sm_ready, 3 * L + 3)
                nc.scalar.activation(pc[:, :, :, :, :], pc[:, :, :, :, :], ACT.Exp, scale=SCALE).then_inc(p_exp, 1)
                act.wait_ge(gate_copied, 12 * L + 12)
                nc.scalar.activation(gates[:, 0:8, :], gates[:, 0:8, :], ACT.Sigmoid).then_inc(gates_ready, 1)
                split_to(base + 22)
                act.wait_ge(pT_done, 3 * L + 3)
                nc.scalar.activation(att[0:CMP_M, :, 0:T].rearrange("p (b a) t -> p b a t", b=2),
                                     psum[0:CMP_M, 0:2, :].rearrange("p b (a t) -> p b a t", a=2), ACT.Copy).then_inc(pT_ready, 1)
                nc.scalar.activation(gates[:, 8:16, :], gates[:, 8:16, :], ACT.Sigmoid).then_inc(gates_ready, 1)
                act.wait_ge(yc_ready, L + 1)
                nc.scalar.activation(y_hi[:, 2, :, :], ysum, ACT.Copy).then_inc(yc_hi, 1)
                split_to(base + 23)
                nc.scalar.activation(gates[:, 16:24, :], gates[:, 16:24, :], ACT.Sigmoid).then_inc(gates_ready, 1)
                split_to(base + 24)
                for b in range(4):
                    act.wait_ge(merged, 4 * L + b + 1)
                    nc.scalar.activation(xT_hi[:, 2 * b:2 * b + 2, :].rearrange("p a t -> p (a t)"),
                                         gates[:, 2 * b:2 * b + 2, :].rearrange("p a t -> p (a t)"), ACT.Copy).then_inc(mg_hi, 1)
                split_to(base + MIX_UNITS + 1)
                norm_roots([h_mixed] * 2, [2 * L + 1, 2 * L + 2])
                if L == 0:
                    transposed(1, 4, xT_hi, xT_hi_ready)

                    def group(g, i, par, w=512):
                        act.wait_ge(unit_used, i * 6 + (FFN_U + max(3 * g, 1)))
                        if not (isinstance(i, int) and g == 0):
                            act.wait_ge(f_hid_ready, i * 2 + g)
                        nc.scalar.activation(f_silu[:, 0:w], psum[:, 4 + 2 * par, 0:w], ACT.Silu).then_inc(f_silu_ready, 1)

                    def high(g, i, par):
                        act.wait_ge(f_hid_ready, i * 2 + (g + 1))
                        nc.scalar.activation(f_hi[:, par, :, :].rearrange("p a t -> p (a t)"), f_hid[:, :], ACT.Copy).then_inc(f_hi_ready, 1)
                    split_to(FFN_U + 3)
                    group(0, 0, 0)
                    high(0, 0, 0)
                    assert at[0] == FFN_U + 4
                    with act.Fori(0, 4) as i:
                        for b in range(2):
                            u = FFN_U + 4 + 3 * b
                            split_hi(act, u, i, 6)
                            group(1 + b, i, (1 + b) % 2)
                            split_hi(act, u + 1, i, 6)
                            high(1 + b, i, (1 + b) % 2)
                            split_hi(act, u + 2, i, 6)
                    at[0] = FFN_U + 28
                    for g in (9, 10):
                        split_to(FFN_U + 3 * g + 1)
                        group(g, 0, g % 2)
                        split_to(FFN_U + 3 * g + 2)
                        high(g, 0, g % 2)
                        split_to(FFN_U + 3 * g + 3)
                    split_to(MIX1_U)

            transposed(3, 4, xTf, xTf_ready)
            split_to(MOE_U + 2)
            act.wait_ge(dv_ready, 1)
            nc.scalar.activation(ex[:, :, 0], ex[:, :, 1], ACT.Exp).then_inc(ex_ready, 1)

            def expert_pass(half, start):
                e0, s0 = EXPERTS * half, EXPERTS * STEPS * half
                def gathered(i, c):
                    act.wait_ge(gather_done, i + (c + 1))
                    nc.scalar.activation(sel_hi[:, :, :].rearrange("p (b k) s -> p b (k s)", b=2), psum[:, 5:7, :], ACT.Copy).then_inc(sel_hi_ready, 1)

                def values(i, c, u):
                    act.wait_ge(unit_used, i * PER_EXPERT + (u + 1))
                    if not (isinstance(i, int) and c + i == 0):
                        act.wait_ge(scatter_done, i + c)
                    nc.scalar.activation(y_e[:, :].rearrange("p (b n) -> p b n", b=2), psum[:, 3:5, :], ACT.Copy).then_inc(y_e_ready, 1)

                def expert(i, first):
                    base = start - 2
                    for j in range(STEPS):
                        n = s0 + j
                        for u in range(base + 6 * j + 2, base + 6 * j + 6):
                            if not first or u >= at[0]:
                                split_hi(act, u, i, PER_EXPERT)
                        act.wait_ge(unit_used, i * PER_EXPERT + (base + 6 * j + 2 + 2 * (first and j == 0)))
                        if not (first and n == 0):
                            act.wait_ge(e_hid_ready, i * STEPS + n)
                        nc.scalar.activation(e_silu[:, :], psum[:, 0, :], ACT.Silu).then_inc(e_silu_ready, 1)
                        split_hi(act, base + 6 * j + 6, i, PER_EXPERT)
                        if first and j == 0:
                            for b in range(4):
                                act.wait_ge(spreadT_done, 4 * half + b + 1)
                                nc.scalar.activation(spread[:, 2 * b:2 * b + 2, :].rearrange("p e t -> p (e t)"),
                                                     psum[:, SPREAD_BANKS[b], :], ACT.Copy).then_inc(spread_ready, 1)
                        if j == STEPS - 1:
                            gathered(i, e0 + half + 1)
                        split_hi(act, base + 6 * j + 7, i, PER_EXPERT)
                        act.wait_ge(e_T, i * STEPS + (n + 1))
                        nc.scalar.activation(eT_hi[:, :, :].rearrange("p a s -> p (a s)"), psum[:, 2, :], ACT.Copy).then_inc(eT_hi_ready, 1)
                        if j == 0 and not first:
                            values(i, e0 - 1, base + 5)
                gathered(0, e0 + half)
                expert(0, True)
                with act.Fori(1, EXPERTS) as i:
                    expert(i, False)
                values(0, e0 + EXPERTS - 1, start + MOE_UNITS - 1)
                load_sqrt()
                act.wait_ge(h_added, EXPERTS * (half + 1))
            expert_pass(0, MOE_U)
            act.wait_ge(most_ready, 1)
            with act.If(act.value_load(most_i[0:1, 0:1], min_val=0, max_val=T) > CAPACITY):
                expert_pass(1, MOE_U + MOE_UNITS)
            nc.scalar.activation(hn[:, 1, :], h[:, 1, :], ACT.Square, accum_out=ssq[:, 1:2]).then_inc(act_sum, 1)
            act.wait_ge(sq_ready, 1)
            root(0)
            act.wait_ge(act_sum, sums[0] + 1)
            root(1)

        @block.vector
        def _(dve):
            at = [0]
            done = [0]
            norms = [0]

            def step(ins):
                done[0] += 1
                ins.then_inc(dve_step, 1)
                dve.wait_ge(dve_step, done[0])

            def split_to(u):
                while at[0] <= u:
                    split_lo(dve, at[0], **odd_shape(at[0]))
                    at[0] += 1
            V = nc.vector

            def norm(n, ready):
                dve.wait_ge(gain_landed, 16 * (n + 1))
                for t in range(TT):
                    dve.wait_ge(rt_ready, 2 * n + t + 1)
                    step(V.reciprocal(rstd[:, t:t + 1], rstd[:, t:t + 1]))
                    for a in range(0, D, 512):
                        V.scalar_tensor_tensor(out=hn[:, t, a:a + 512], in0=h[:, t, a:a + 512], scalar=rstd[:, t:t + 1],
                                               in1=gain[:, a:a + 512], op0=ALU.mult, op1=ALU.mult).then_inc(ready, 1)

            def transposed_lo(n, bank):
                for b in range(4):
                    dve.wait_ge(xT_hi_ready, 4 * n + b + 1)
                    k = 4 * (b % 2)
                    o = (slice(None), slice(k, k + 4), slice(b // 2 * P, (b // 2 + 1) * P))
                    V.tensor_tensor(xT_lo[o], psum[:, bank + b, :].rearrange("p (k t) -> p k t", k=4),
                                    xT_hi[o].bitcast(F32), ALU.subtract).then_inc(xT_ready, 1)
                    if n == 0 and b == 1:
                        split_to(0)

            def add_tile(t, psum_bank):
                return V.tensor_tensor(h[:, t, :].rearrange("p (b n) -> p b n", b=2), h[:, t, :].rearrange("p (b n) -> p b n", b=2),
                                       psum[:, psum_bank:psum_bank + 2, :], ALU.add)

            for L in range(LAYERS):
                base = MIX1_U * L
                if L == 0:
                    for t in range(TT):
                        dve.wait_ge(x_landed[t], 16)
                norm(2 * L, hn_ready)
                transposed_lo(2 * L, 0)
                split_to(base + 7)
                if L == 0:
                    dve.wait_ge(rope_landed, 16)
                    dve.wait_ge(small_T_ready, 1)
                dve.wait_ge(tokB_ready, L + 1)
                dve.wait_ge(tokA_ready, L + 1)
                tmp = small[:, 64:64 + 2 * 2 * 4 * 8 * 1].rearrange("p (a t h c) -> p a t h c", a=2, t=TT, h=4)
                for k, (c0, stride, count) in enumerate(((256, HD, 4), (512, 2 * HD, 3))):
                    grp = tok[:, :, c0:c0 + stride * count].rearrange("p t (h c) -> p t h c", h=count)
                    x1, x2 = grp[:, :, :, 0:8], grp[:, :, :, 8:16]
                    cos, nsin, sin = (bc(rope_sb[:, :, a, :], 2, count) for a in range(3))
                    b1, b2 = tmp[:, 0, :, 0:count, :], tmp[:, 1, :, 0:count, :]
                    V.tensor_tensor(b1, x2, nsin, ALU.mult)
                    step(V.tensor_tensor(b2, x1, sin, ALU.mult))
                    V.tensor_tensor(x1, x1, cos, ALU.mult)
                    step(V.tensor_tensor(x2, x2, cos, ALU.mult))
                    V.tensor_tensor(x1, x1, b1, ALU.add)
                    last = V.tensor_tensor(x2, x2, b2, ALU.add)
                    if k:
                        last.then_inc(roped, 1)
                    else:
                        step(last)
                split_to(base + 8)
                dve.wait_ge(uv_ready, L + 1)
                for t in range(TT):
                    last = V.tensor_tensor_reduce(out=att[:, t, 0:256], in0=uv[:, t, 256:512], in1=uv[:, t, 256:512], scale=1.0, scalar=0.0,
                                                  op0=ALU.mult, op1=ALU.add, accum_out=small[:, t:t + 1])
                last.then_inc(vsq_ready, 1)
                dve.wait_ge(z_done, L + 1)
                V.tensor_scalar(sc, psum[:, 4:8, 0:384], SCALE, None, ALU.mult).then_inc(zs_ready, 1)
                split_to(base + 10)
                dve.wait_ge(soft_ready, 3 * L + 3)
                step(V.scalar_tensor_tensor(out=att[:, :, :], in0=sc, scalar=0.0, in1=att[:, :, :], op0=ALU.max, op1=ALU.add))
                V.tensor_tensor(sc, sc, att[:, :, :], ALU.subtract).then_inc(sp_ready, 1)
                split_to(base + 11)
                dve.wait_ge(kT_ready, L + 1)
                for half in range(2):
                    rows = slice(HD * half, HD * half + HD)
                    for c8 in range(2):
                        src = kT[rows, 0:2, :].rearrange("p v (m l) -> p v l m", l=16)[:, :, half:16:2, c8:c8 + CMP_M]
                        pos = posT[rows, 32 * L:32 * L + 32].rearrange("p (v c) -> p v c", v=2)[:, :, 8 * c8:8 * c8 + 8]
                        last = V.tensor_tensor(blk[rows, :, 8 * c8:8 * c8 + 8, :], src, bc(pos, 3, CMP_M), ALU.add)
                last.then_inc(blk_ready, 1)
                dve.wait_ge(vrt_ready, L + 1)
                step(V.reciprocal(small[:, 4:6], small[:, 2:4]))
                dve.wait_ge(sgug_landed, 16 * (L + 1))
                for t in range(TT):
                    last = V.scalar_tensor_tensor(out=uv[:, t, 256:512], in0=uv[:, t, 256:512], scalar=small[:, 4 + t:5 + t],
                                                  in1=sgu_g[:, :], op0=ALU.mult, op1=ALU.mult)
                last.then_inc(vn_ready, 1)
                split_to(base + 12)
                dve.wait_ge(btw_done, L + 1)
                V.tensor_tensor(sc, sc, psum[:, 4:8, 0:384], ALU.subtract).then_inc(arg_ready, 1)
                split_to(base + 14)
                dve.wait_ge(mix_done, L + 1)
                mix = psum[:, 3, :].rearrange("p (t g d) -> p t g d", t=TT, g=4)
                for t in range(TT):
                    last = V.tensor_tensor(uv[:, t, 256:512].rearrange("p (g d) -> p g d", g=4), mix[:, t, :, :],
                                           bc(biasT[:, L, :], 2, HD), ALU.add)
                step(last)
                V.tensor_tensor(uv[:, :, 0:256], uv[:, :, 0:256], uv[:, :, 256:512], ALU.mult).then_inc(ya_ready, 1)
                split_to(base + 15)
                dve.wait_ge(yb_hi, L + 1)
                V.tensor_tensor(y_lo[:, 1, :, :].rearrange("p a t -> p (a t)"), psum[:, 4, :],
                                y_hi[:, 1, :, :].rearrange("p a t -> p (a t)").bitcast(F32), ALU.subtract).then_inc(y_ready, 1)
                split_to(base + 16)

                def scores(n):
                    dve.wait_ge(s_done, 3 * L + n + 1)
                    step(V.tensor_tensor(sc, psum[:, 4:8, 0:384], bc(causal[:, :, :].rearrange("p b k -> p (b k)"), 1, HEADS), ALU.add))
                    V.tensor_reduce(small[:, 40:44], sc[:, :, 0:P], AX_X, ALU.max)
                    step(V.tensor_reduce(small[:, 44:48], sc[:, :, P:3 * P], AX_X, ALU.max))
                    V.tensor_scalar(small[:, 48:56], small[:, 40:48], -SCALE, None, ALU.mult).then_inc(sm_ready, 1)

                def weights(n, branch):
                    dve.wait_ge(p_exp, 3 * L + n + 1)
                    dve.wait_ge(gsig, L + 1)
                    step(V.reciprocal(small[:, 128:136], small[:, 56:64]))
                    g = small[:, 16:40].rearrange("p (t h b) -> p t h b", t=TT, b=3)[:, :, :, branch]
                    step(V.tensor_tensor(small[:, 136:144].rearrange("p (t h) -> p t h", t=TT), small[:, 128:136].rearrange("p (t h) -> p t h", t=TT), g, ALU.mult))
                    V.tensor_tensor(sc[:, :, 0:P], sc[:, :, 0:P], bc(small[:, 136:140], 2, P), ALU.mult)
                    V.tensor_tensor(sc[:, :, P:3 * P], sc[:, :, P:3 * P], bc(small[:, 140:144], 2, 2 * P), ALU.mult).then_inc(p_ready, 1)
                scores(0)
                weights(0, 1)
                split_to(base + 17)
                split_to(base + 18)
                dve.wait_ge(ya_hi, L + 1)
                V.tensor_tensor(y_lo[:, 0, :, :].rearrange("p a t -> p (a t)"), psum[:, 2, :],
                                y_hi[:, 0, :, :].rearrange("p a t -> p (a t)").bitcast(F32), ALU.subtract).then_inc(y_ready, 1)
                dve.wait_ge(av_done, 3 * L + 1)
                V.tensor_copy(ysum.rearrange("p a t -> p (a t)"), psum[:, 2, :]).then_inc(av_added, 1)
                scores(1)
                split_to(base + 19)
                weights(1, 2)
                split_to(base + 21)
                dve.wait_ge(av_done, 3 * L + 2)
                dve.wait_ge(av_added, 2 * L + 1)
                V.tensor_tensor(ysum.rearrange("p a t -> p (a t)"), ysum.rearrange("p a t -> p (a t)"), psum[:, 2, :], ALU.add).then_inc(av_added, 1)
                dve.wait_ge(s_done, 3 * L + 3)
                pcf = pc[:, :, :, :, :].rearrange("p a t j m -> p (a t j) m")
                for half in range(2):
                    last = V.tensor_tensor(pc[:, half, :, :, :], psum[:, half, 0:64].rearrange("p (t j m) -> p t j m", t=TT, j=2)[:, :, :, 0:CMP_M],
                                           bc(cmp_mask[:, :, :], 2, 2), ALU.add)
                step(last)
                step(V.tensor_reduce(small[:, 144:152], pcf, AX_X, ALU.max))
                step(V.tensor_scalar(small[:, 152:160], small[:, 144:152], NEG / 10, None, ALU.max))
                V.tensor_tensor(pcf, pcf, bc(small[:, 152:160], 2, CMP_M), ALU.subtract).then_inc(sm_ready, 1)
                dve.wait_ge(p_exp, 3 * L + 3)
                step(V.tensor_reduce(small[:, 160:168], pcf, AX_X, ALU.add))
                step(V.tensor_scalar(small[:, 168:176], small[:, 160:168], 1e-30, None, ALU.max))
                step(V.reciprocal(small[:, 176:184], small[:, 168:176]))
                for half in range(2):
                    g = small[:, 16:40].rearrange("p (t j a b) -> p t j a b", t=TT, j=2, b=3)[:, :, :, half, 0]
                    last = V.tensor_tensor(small[:, 184 + 4 * half:188 + 4 * half].rearrange("p (t j) -> p t j", t=TT),
                                           small[:, 176 + 4 * half:180 + 4 * half].rearrange("p (t j) -> p t j", t=TT), g, ALU.mult)
                step(last)
                V.tensor_tensor(pcf, pcf, bc(small[:, 184:192], 2, CMP_M), ALU.mult).then_inc(p_ready, 1)
                def gated_branch(n, b):
                    if b < 3:
                        dve.wait_ge(br_done, 9 * L + 3 * n + b + 1)
                    else:
                        dve.wait_ge(unit_used, base + 21 + n)
                    g = gates[:, 8 * n + 2 * b:8 * n + 2 * b + 2, :].rearrange("p a t -> p (a t)")
                    V.tensor_tensor(g, g, psum[:, 4 + b, :], ALU.mult).then_inc(br_used, 1)

                def merged_lo(b):
                    dve.wait_ge(mg_hi, 4 * L + b + 1)
                    o = (slice(None), slice(2 * b, 2 * b + 2), slice(None))
                    V.tensor_tensor(xT_lo[o].rearrange("p a t -> p (a t)"), gates[o].rearrange("p a t -> p (a t)"),
                                    xT_hi[o].rearrange("p a t -> p (a t)").bitcast(F32), ALU.subtract).then_inc(mg_ready, 1)
                dve.wait_ge(gates_ready, 3 * L + 1)
                for b in range(4):
                    gated_branch(0, b)
                split_to(base + 22)
                dve.wait_ge(av_done, 3 * L + 3)
                dve.wait_ge(av_added, 2 * L + 2)
                V.tensor_tensor(ysum.rearrange("p a t -> p (a t)"), ysum.rearrange("p a t -> p (a t)"), psum[:, 2, :], ALU.add).then_inc(yc_ready, 1)
                dve.wait_ge(gates_ready, 3 * L + 2)
                gated_branch(1, 0)
                dve.wait_ge(yc_hi, L + 1)
                V.tensor_tensor(y_lo[:, 2, :, :], ysum, y_hi[:, 2, :, :].bitcast(F32), ALU.subtract).then_inc(y_ready, 1)
                gated_branch(1, 1)
                for b in range(2, 4):
                    gated_branch(1, b)
                split_to(base + 23)
                dve.wait_ge(gates_ready, 3 * L + 3)
                for b in range(4):
                    gated_branch(2, b)
                    if b == 3:
                        split_to(base + 24)
                    if b:
                        merged_lo(b - 1)
                merged_lo(3)
                split_to(base + MIX_UNITS + 1)
                dve.wait_ge(tile0_done, 2 * L + 1)
                add_tile(0, 0).then_inc(h_mixed, 1)
                dve.wait_ge(unit_used, base + MIX_UNITS)
                add_tile(1, 2).then_inc(h_mixed, 1)
                dve.wait_ge(h_mixed, 2 * L + 2)
                norm(2 * L + 1, hn_ready)
                if L == 0:
                    transposed_lo(1, 4)

                    def group(g, i, par, w=512):
                        if not (isinstance(i, int) and g == 0):
                            dve.wait_ge(f_lo_ready, i * 2 + g)
                        dve.wait_ge(f_silu_ready, i * 2 + (g + 1))
                        dve.wait_ge(unit_used, i * 6 + (FFN_U + max(3 * g + 1, 2)))
                        V.tensor_tensor(f_hid[:, 0:w], f_silu[:, 0:w], psum[:, 5 + 2 * par, 0:w], ALU.mult).then_inc(f_hid_ready, 1)

                    def low(g, i, par):
                        dve.wait_ge(f_hi_ready, i * 2 + (g + 1))
                        V.tensor_tensor(f_lo[:, par, :, :].rearrange("p a t -> p (a t)"), f_hid[:, :],
                                        f_hi[:, par, :, :].rearrange("p a t -> p (a t)").bitcast(F32), ALU.subtract).then_inc(f_lo_ready, 1)
                    split_to(FFN_U + 3)
                    group(0, 0, 0)
                    low(0, 0, 0)
                    with dve.Fori(0, 4) as i:
                        for b in range(2):
                            u = FFN_U + 4 + 3 * b
                            split_lo(dve, u, i, 6)
                            group(1 + b, i, (1 + b) % 2)
                            split_lo(dve, u + 1, i, 6)
                            low(1 + b, i, (1 + b) % 2)
                            split_lo(dve, u + 2, i, 6)
                    at[0] = FFN_U + 28
                    for g in (9, 10):
                        split_to(FFN_U + 3 * g + 1)
                        group(g, 0, g % 2)
                        split_to(FFN_U + 3 * g + 2)
                        low(g, 0, g % 2)
                        split_to(FFN_U + 3 * g + 3)
                    split_to(MIX1_U)
                    dve.wait_ge(tile0_done, 2)
                    add_tile(0, 0).then_inc(h_ffn, 1)
                    dve.wait_ge(unit_used, MIX1_U)
                    add_tile(1, 2).then_inc(h_ffn, 1)
                    dve.wait_ge(h_ffn, 2)

            split_to(MOE_U + 2)
            dve.wait_ge(lg_done, 1)
            dve.wait_ge(consts, 2)
            step(V.tensor_copy(lg[:, :, :], psum[:, 0, 0:16].rearrange("p (t e) -> p t e", t=TT)))
            for t in range(TT):
                last = V.max(top_v[:, t, :], lg[:, t, :])
            step(last)
            for t in range(TT):
                last = V.max_index(top_i[:, t, :], top_v[:, t, :], lg[:, t, :])
            step(last)
            V.tensor_tensor(ex[:, :, 1], top_v[:, :, 1], top_v[:, :, 0], ALU.subtract).then_inc(dv_ready, 1)
            step(V.tensor_copy(top_f[:, :, :], top_i[:, :, 0:2]))
            for n in range(2):
                last = V.tensor_tensor(hit[:, n, :, :], bc(slot_no[:, 0:EXPERTS], 1, TT), bc(top_f[:, :, n], 2, EXPERTS), ALU.is_equal)
            step(last)
            V.tensor_tensor(chosen[:, :, :], hit[:, 0, :, :], hit[:, 1, :, :], ALU.add).then_inc(chosen_ready, 1)
            dve.wait_ge(ex_ready, 1)
            step(V.tensor_scalar(ex[:, :, 1], ex[:, :, 0], 1.0, None, ALU.add))
            step(V.reciprocal(ex[:, :, 1], ex[:, :, 1]))
            dve.wait_ge(pos_done, 1)
            step(V.scalar_tensor_tensor(out=place[:, :, :], in0=psum[:, 1, 0:16].rearrange("p (t e) -> p t e", t=TT), scalar=1.0,
                                        in1=chosen[:, :, :], op0=ALU.add, op1=ALU.mult))

            def expert_pass(half, start, step):
                e0, s0 = EXPERTS * half, EXPERTS * STEPS * half
                if half:
                    dve.wait_ge(h_added, EXPERTS)
                    step(V.tensor_scalar(place[:, :, :], place[:, :, :], float(-CAPACITY), None, ALU.add))
                def gathered(i, c):
                    dve.wait_ge(sel_hi_ready, i + (c + 1))
                    V.tensor_tensor(sel_lo[:, :, :].rearrange("p (b k) s -> p b (k s)", b=2), psum[:, 5:7, :],
                                    sel_hi[:, :, :].rearrange("p (b k) s -> p b (k s)", b=2).bitcast(F32), ALU.subtract).then_inc(sel_ready, 1)

                V.scalar_tensor_tensor(out=pick[:, 0, :, :], in0=bc(place[:, :, 0], 2, P), scalar=-1.0, in1=bc(slot_no[:, :], 1, TT),
                                       op0=ALU.add, op1=ALU.is_equal).then_inc(pick_ready, 1)
                for c in range(TT):
                    last = V.scalar_tensor_tensor(out=pick[:, 1:EXPERTS, c, :], in0=bc(place[:, c, 1:EXPERTS], 2, P), scalar=-1.0,
                                                  in1=bc(slot_no[:, :], 1, EXPERTS - 1), op0=ALU.add, op1=ALU.is_equal)
                last.then_inc(pick_ready, 1)
                gathered(0, e0 + half)
                if not half:
                    step(V.tensor_tensor(ex[:, :, 0], ex[:, :, 0], ex[:, :, 1], ALU.mult))
                    for n in range(2):
                        last = V.tensor_tensor(hit[:, n, :, :], hit[:, n, :, :], bc(ex[:, :, 1 - n], 2, EXPERTS), ALU.mult)
                    step(last)
                    step(V.tensor_tensor(gate[:, :, :], hit[:, 0, :, :], hit[:, 1, :, :], ALU.add))
                dve.wait_ge(pick_ready, 2 * half + 2)
                for c in range(TT):
                    last = V.tensor_tensor(gated[:, :, c, :], pick[:, 0:EXPERTS, c, :], bc(gate[:, c, :], 2, P), ALU.mult)
                last.then_inc(gated_ready, 1)

                def add(i, c):
                    for t, scattered in enumerate((tile0_scattered, scatter_done)):
                        dve.wait_ge(scattered, i + (c + 1))
                        for n in range(2):
                            bank = (5, 6, 7, 2)[2 * t + n]
                            hh = h[:, t, 512 * n:512 * n + 512]
                            last = V.tensor_tensor(hh, hh, psum[:, bank, :], ALU.add)
                    last.then_inc(h_added, 1)

                def expert(i, first):
                    base = start - 2
                    for j in range(STEPS):
                        n = s0 + j
                        for u in range(base + 6 * j + 2, base + 6 * j + 6):
                            if not first or u >= at[0]:
                                split_lo(dve, u, i, PER_EXPERT)
                        if first and j == 0:
                            split_lo(dve, base + 6, i, PER_EXPERT)
                        dve.wait_ge(e_silu_ready, i * STEPS + (n + 1))
                        dve.wait_ge(unit_used, i * PER_EXPERT + (base + 6 * j + 4 + 2 * (first and j == 0)))
                        if not (first and n == 0):
                            dve.wait_ge(e_T, i * STEPS + n)
                        V.tensor_tensor(e_hid[:, :], e_silu[:, :], psum[:, 1, :], ALU.mult).then_inc(e_hid_ready, 1)
                        if not first or j:
                            split_lo(dve, base + 6 * j + 6, i, PER_EXPERT)
                        if j == STEPS - 1:
                            gathered(i, e0 + half + 1)
                        if j == 1 and not first:
                            add(i, e0 - 1)
                        if j < STEPS - 1:
                            split_lo(dve, base + 6 * j + 7, i, PER_EXPERT)
                        dve.wait_ge(eT_hi_ready, i * STEPS + (n + 1))
                        V.tensor_tensor(eT_lo[:, :, :].rearrange("p a s -> p (a s)"), psum[:, 2, :],
                                        eT_hi[:, :, :].rearrange("p a s -> p (a s)").bitcast(F32), ALU.subtract).then_inc(eT_ready, 1)
                        if j == STEPS - 1:
                            split_lo(dve, base + 6 * j + 7, i, PER_EXPERT)
                if not half:
                    step(V.tensor_reduce(most[:, :], psum[:, 1, 16:24], AX_X, ALU.max))
                    V.tensor_copy(most_i[:, :], most[:, :]).then_inc(most_ready, 1)
                expert(0, True)
                with dve.Fori(1, EXPERTS) as i:
                    expert(i, False)
                add(0, e0 + EXPERTS - 1)
                dve.wait_ge(h_added, EXPERTS * (half + 1))
            expert_pass(0, MOE_U, step)
            with dve.If(dve.value_load(most_i[0:1, 0:1], min_val=0, max_val=T) > CAPACITY):
                rest = [0]

                def rest_of(ins):
                    rest[0] += 1
                    ins.then_inc(rest_step, 1)
                    dve.wait_ge(rest_step, rest[0])
                expert_pass(1, MOE_U + MOE_UNITS, rest_of)
            V.tensor_tensor_reduce(out=hn[:, 0, :], in0=h[:, 0, :], in1=h[:, 0, :], scale=1.0, scalar=0.0,
                                   op0=ALU.mult, op1=ALU.add, accum_out=ssq[:, 0:1]).then_inc(sq_ready, 1)
            dve.wait_ge(sq_ready, 1)
            norm(4, out_ready)

        @block.tensor
        def _(pe):
            M = nc.tensor

            def keep_clock(count):
                for _ in range(count):
                    M.matmul(psum[:, 7, 384:512], ident[:, :], ident[:, :], start=True, stop=True)

            def transpose_hn(n, bank):
                for b in range(4):
                    t, k = b // 2, 4 * (b % 2)
                    pe.wait_ge(hn_ready, 4 * n + b + 1)
                    for a in range(4):
                        last = M.transpose(psum[:, bank + b, a * P:(a + 1) * P], hn[:, t, (k + a) * P:(k + a + 1) * P], ident[:, :])
                    last.then_inc(hnT_done, 1)

            def rows(u, chunks, bank, n=UNIT):
                w = unit(pe, u, KC, n=n)
                for c in range(chunks):
                    width = min(P, n // KC - c * P)
                    for k in range(KC):
                        last = mm3(psum[0:width, bank, c * T:(c + 1) * T], [a[:, k, c * P:c * P + width] for a in w],
                                   [a[:, k, :] for a in xT], k == 0, k == KC - 1)
                return last

            def tokens(u, width, bank):
                for half in range(2):
                    w = unit(pe, u + half, 4, n=4 * width)
                    for t in range(TT):
                        for k in range(4):
                            kk = 4 * half + k
                            last = mm3(psum[:, bank + t, 0:width], [a[:, kk, t * P:(t + 1) * P] for a in xT],
                                       [a[:, k, :] for a in w], kk == 0, kk == KC - 1)
                    last.then_inc(unit_used, 1)

            pe.wait_ge(consts, 1)
            for L in range(LAYERS):
                base = MIX1_U * L
                keep_clock(12 if L else 9)
                transpose_hn(2 * L, 0)
                pe.wait_ge(xT_ready, 8 * L + 4)
                for n in range(2):
                    rows(base + n, 2, 4 + n).then_inc(unit_used, 1)
                if L == 0:
                    pe.wait_ge(posb_landed, 32)
                    M.transpose(psum[:, 3, 0:64], pos_b, ident[0:64, 0:64])
                    M.transpose(psum[:, 3, 64:72], sb_b, ident[0:8, 0:8]).then_inc(small_T, 1)
                for n, (width, bank) in enumerate(((512, 6), (CKV_N, 0), (512, 2))):
                    if L == 0 and n == 2:
                        pe.wait_ge(small_T_ready, 1)
                    tokens(base + 2 + 2 * n, width, bank)

                def gate_unit(n):
                    if n >= 2:
                        pe.wait_ge(gate_copied, 12 * L + n - 1)
                    else:
                        pe.wait_ge(tokB_ready, L + 1)
                    rows(base + 8 + n, 2, n % 2).then_inc(unit_used, 1)

                pe.wait_ge(sbT_ready, L + 1)
                pe.wait_ge(tokA_ready, L + 1)
                for hh in range(HEADS):
                    r, j = slice(HD * (hh % 2), HD * (hh % 2) + HD), hh // 2
                    M.matmul(psum[:, 4 + hh, 0:T], sbT[r, 2 + j, 0:P], sbT[r, j, :], start=True, stop=True)
                    last = M.matmul(psum[:, 4 + hh, T:T + P], sbT[r, 2 + j, P:T], sbT[r, j, P:T], start=True, stop=True)
                last.then_inc(z_done, 1)
                gate_unit(0)
                gate_unit(1)
                pe.wait_ge(dup_ready, L + 1)
                pe.wait_ge(uv_ready, L + 1)
                for k in range(4):
                    for t in range(TT):
                        c = (k % 2) * T + t * P
                        last = M.transpose(psum[:, 2 + k // 2, c:c + P], dup[:, t, k, :], ident[:, :])
                last.then_inc(kTp_done, 1)
                gate_unit(2)
                pe.wait_ge(sp_cut, L + 1)
                for hh in range(HEADS):
                    M.matmul(psum[:, 4 + hh, 0:T], later[:, :], att[:, hh, 0:T], start=True, stop=False)
                    M.matmul(psum[:, 4 + hh, P:T], ones[:, :], att[:, hh, T:T + P], start=False, stop=True)
                    last = M.matmul(psum[:, 4 + hh, T:T + P], later[:, :], att[:, hh, T:T + P], start=True, stop=True)
                last.then_inc(btw_done, 1)
                pe.wait_ge(kT_ready, L + 1)
                for a in range(2):
                    for t in range(TT):
                        last = M.transpose(psum[:, 2, a * T + t * P:a * T + (t + 1) * P], tok[:, t, 256 + a * P:256 + (a + 1) * P], ident[:, :])
                last.then_inc(qTp_done, 1)
                pe.wait_ge(sguw_landed, 16 * (L + 1))
                for g in range(4):
                    last = M.transpose(psum[:, 3, g * P:(g + 1) * P], sgu_raw[:, g, :], ident[:, :])
                last.then_inc(sguTp_done, 1)
                gate_unit(3)

                def hidden(v):
                    for c in range(CMP_C):
                        last = M.matmul(psum[0:CMP_M, 2 + v, 0:256], blk[:, v, c, :], w1[:, c, :], start=c == 0, stop=c == CMP_C - 1)
                    last.then_inc(ck_done, 1)

                def hidden_T(v):
                    pe.wait_ge(hc_ready, 2 * L + v + 1)
                    for a in range(2):
                        last = M.transpose(psum[:, 2 + v, 16 * a:16 * a + CMP_M], hid_c[:, v, a * P:(a + 1) * P], ident[0:CMP_M, 0:CMP_M])
                    last.then_inc(hcT_done, 1)
                pe.wait_ge(blk_ready, L + 1)
                pe.wait_ge(qT_ready, L + 1)
                pe.wait_ge(w1_landed, 32 * L + 16)
                hidden(0)
                pe.wait_ge(vn_ready, L + 1)
                pe.wait_ge(sguT_cut, L + 1)
                for g in range(4):
                    o = psum[:, 3, :].rearrange("p (t c) -> p t c", t=TT)[:, :, g * HD:(g + 1) * HD]
                    last = M.matmul(o, sgu_T[:, g, :], uv[:, :, 256 + g * HD:256 + (g + 1) * HD], start=True, stop=True)
                last.then_inc(mix_done, 1)
                gate_unit(4)
                pe.wait_ge(aT_ready, L + 1)
                for hh in range(HEADS):
                    r, j = slice(HD * (hh % 2), HD * (hh % 2) + HD), hh // 2
                    M.matmul(psum[r, 4, j * T:(j + 1) * T], tok[:, 0, hh * HD:(hh + 1) * HD], sc[:, hh, 0:T], start=True, stop=False)
                    last = M.matmul(psum[r, 4, j * T + P:(j + 1) * T], tok[:, 1, hh * HD:(hh + 1) * HD], sc[:, hh, T:T + P], start=False, stop=True)
                last.then_inc(yb_done, 1)

                def scores(n):
                    if n == 0:
                        pe.wait_ge(y_ready, 3 * L + 1)
                    else:
                        pe.wait_ge(pT_ready, 3 * L + 1)
                    for hh in range(HEADS):
                        r, j = slice(HD * (hh % 2), HD * (hh % 2) + HD), hh // 2
                        M.matmul(psum[:, 4 + hh, 0:P], qT[r, j, 0:P], kT[r, 2 + n, 0:P], start=True, stop=True)
                        last = M.matmul(psum[:, 4 + hh, P:3 * P], qT[r, j, P:T], kT[r, 2 + n, :], start=True, stop=True)
                    last.then_inc(s_done, 1)

                def weights_T(n):
                    pe.wait_ge(p_ready, 3 * L + n + 1)
                    for hh in range(HEADS):
                        for b in range(3):
                            last = M.transpose(psum[:, 4 + hh, b * P:(b + 1) * P], sc[:, hh, b * P:(b + 1) * P], ident[:, :])
                    last.then_inc(pT_done, 1)

                def outputs(n, c0):
                    pe.wait_ge(pT_ready, 3 * L + n + 1)
                    if n == 0:
                        pe.wait_ge(y_ready, 3 * L + 2)
                    else:
                        pe.wait_ge(av_added, 2 * L + n)
                    for hh in range(HEADS):
                        r, j = slice(HD * (hh % 2), HD * (hh % 2) + HD), hh // 2
                        M.matmul(psum[r, 2, j * T:(j + 1) * T], tok[:, 0, c0:c0 + HD], att[:, hh, 0:T], start=True, stop=False)
                        last = M.matmul(psum[r, 2, j * T + P:(j + 1) * T], tok[:, 1, c0:c0 + HD], att[:, hh, T:T + P], start=False, stop=True)
                    last.then_inc(av_done, 1)
                hidden_T(0)
                gate_unit(5)
                scores(0)
                pe.wait_ge(ya_ready, L + 1)
                pe.wait_ge(w1_landed, 32 * L + 32)
                hidden(1)
                hidden_T(1)
                pe.wait_ge(hcT_ready, 2 * L + 1)
                pe.wait_ge(w2_landed, 48 * (L + 1))
                for a in range(2):
                    last = M.matmul(psum[:, 2, 64:64 + CMP_M], w2k[:, a, :], hid_cT[:, 0, a, :], start=a == 0, stop=a == 1)
                last.then_inc(kc_done, 1)
                gate_unit(6)
                pe.wait_ge(hcT_ready, 2 * L + 2)
                for a in range(2):
                    last = M.matmul(psum[0:CMP_M, 3, 64:64 + HD], hid_cT[:, 1, a, :], w2v[:, a, :], start=a == 0, stop=a == 1)
                last.then_inc(kc_done, 1)
                pe.wait_ge(kc_ready, 2 * L + 1)
                for a in range(2):
                    for t in range(TT):
                        last = M.transpose(psum[:, 2, a * T + t * P:a * T + (t + 1) * P], uv[:, t, a * P:(a + 1) * P], ident[:, :])
                last.then_inc(yaT_done, 1)
                gate_unit(7)
                weights_T(0)
                gate_unit(8)
                outputs(0, 512 + 3 * HD)
                scores(1)
                gate_unit(9)
                gate_unit(10)
                weights_T(1)
                gate_unit(11)
                outputs(1, 512 + 5 * HD)
                pe.wait_ge(gate_copied, 12 * L + 12)
                for half in range(2):
                    r = slice(HD * half, HD * half + HD)
                    for t in range(TT):
                        for j in range(2):
                            c = 16 * (2 * t + j)
                            last = M.matmul(psum[:, half, c:c + CMP_M], qT[r, j, t * P:(t + 1) * P], kcT[r, :], start=True, stop=True)
                last.then_inc(s_done, 1)

                def outputs_c():
                    pe.wait_ge(pT_ready, 3 * L + 3)
                    pe.wait_ge(av_added, 2 * L + 2)
                    for hh in range(HEADS):
                        r, j = slice(HD * (hh % 2), HD * (hh % 2) + HD), hh // 2
                        last = M.matmul(psum[r, 2, j * T:(j + 1) * T], vc[:, :], att[0:CMP_M, hh, 0:T], start=True, stop=True)
                    last.then_inc(av_done, 1)

                def branch(n):
                    w = unit(pe, base + 20 + n, 2)
                    for dc in range(KC):
                        if n == 1 and dc == KC // 2:
                            outputs_c()
                        if n and dc % 2 == 0:
                            pe.wait_ge(br_used, 12 * L + 4 * (n - 1) + dc // 2 + 1)
                        for k in range(2):
                            last = mm3(psum[:, 4 + dc // 2, (dc % 2) * T:(dc % 2 + 1) * T],
                                       [a[:, k, dc * P:(dc + 1) * P] for a in w], [y_hi[:, n, k, :], y_lo[:, n, k, :]], k == 0, k == 1)
                        if dc % 2 and dc < KC - 1:
                            last.then_inc(br_done, 1)
                    last.then_inc(unit_used, 1)
                branch(0)
                pe.wait_ge(p_ready, 3 * L + 3)
                for half in range(2):
                    for t in range(TT):
                        for j in range(2):
                            hh = 2 * j + half
                            c = (hh % 2) * T + t * P
                            last = M.transpose(psum[0:CMP_M, hh // 2, c:c + P], pc[:, half, t, j, :], ident[:, :])
                last.then_inc(pT_done, 1)
                branch(1)
                pe.wait_ge(y_ready, 3 * L + 3)
                branch(2)
                for n in range(4):
                    pe.wait_ge(mg_ready, 4 * L + n + 1)
                    w = unit(pe, base + 23 + n, 2)
                    for t in range(TT):
                        for k in range(2):
                            kk = 2 * n + k
                            for b in range(2):
                                last = mm3(psum[:, 2 * t + b, :], [a[:, kk, t * P:(t + 1) * P] for a in xT],
                                           [a[:, k, b * 512:(b + 1) * 512] for a in w], kk == 0, kk == KC - 1)
                        if n == 3 and t == 0:
                            last.then_inc(tile0_done, 1)
                    last.then_inc(unit_used, 1)
                keep_clock(12)
                transpose_hn(2 * L + 1, 4)
                if L == 0:
                    pe.wait_ge(xT_ready, 8)

                    def gate_up(g, i, par, u, every, n=UNIT):
                        if not (isinstance(i, int) and g < 2):
                            pe.wait_ge(f_hid_ready, i * 2 + (g - 1))
                        for k2, bank in enumerate((4 + 2 * par, 5 + 2 * par)):
                            w = unit(pe, u + k2, KC, i, every, n=n)
                            for c in range(2):
                                width = min(P, n // KC - c * P)
                                for k in range(KC):
                                    last = mm3(psum[0:width, bank, c * T:(c + 1) * T], [a[:, k, c * P:c * P + width] for a in w],
                                               [a[:, k, :] for a in xT], k == 0, k == KC - 1)
                            last.then_inc(unit_used, 1)

                    def down(g, i, par, u, every, first=False):
                        pe.wait_ge(f_lo_ready, i * 2 + (g + 1))
                        w = unit(pe, u, 2, i, every)
                        for c in range(2):
                            for t in range(TT):
                                for b in range(2):
                                    last = mm3(psum[:, 2 * t + b, :], [f[:, par, c, t * P:(t + 1) * P] for f in (f_hi, f_lo)],
                                               [a[:, c, b * 512:(b + 1) * 512] for a in w], first and c == 0, False)
                        last.then_inc(unit_used, 1)
                    gate_up(0, 0, 0, FFN_U, 6)
                    gate_up(1, 0, 1, FFN_U + 2, 6)
                    down(0, 0, 0, FFN_U + 4, 6, True)
                    gate_up(2, 0, 0, FFN_U + 5, 6)
                    down(1, 0, 1, FFN_U + 7, 6)
                    with pe.Fori(1, 4) as i:
                        for b in range(2):
                            gate_up(1 + b, i, (1 + b) % 2, FFN_U + 2 + 3 * b, 6)
                            down(b, i, b % 2, FFN_U + 4 + 3 * b, 6)
                    gate_up(9, 0, 1, FFN_U + 26, 6)
                    down(8, 0, 0, FFN_U + 28, 6)
                    gate_up(10, 0, 0, FFN_U + 29, 6, n=KC * FT)
                    down(9, 0, 1, FFN_U + 31, 6)
                    pe.wait_ge(f_lo_ready, 11)
                    for c, parts in enumerate((P, FT - P)):
                        w = unit(pe, FFN_U + 32 + c, 1, parts=parts, n=D)
                        for t in range(TT):
                            for b in range(2):
                                last = mm3(psum[:, 2 * t + b, :], [f[0:parts, 0, c, t * P:(t + 1) * P] for f in (f_hi, f_lo)],
                                           [a[:, 0, b * 512:(b + 1) * 512] for a in w], False, c == 1)
                            if c and t == 0:
                                last.then_inc(tile0_done, 1)
                        last.then_inc(unit_used, 1)

            pe.wait_ge(rw_landed, 16)
            for t in range(TT):
                pe.wait_ge(xTf_ready, 2 * t + 2)
                for k in range(KC):
                    last = M.matmul(psum[:, 0, t * 8:t * 8 + 8], xTf[:, k, t * P:(t + 1) * P], rw[:, k, :], start=k == 0, stop=k == KC - 1)
            last.then_inc(lg_done, 1)
            keep_clock(7)
            pe.wait_ge(chosen_ready, 1)
            M.matmul(psum[:, 1, 0:16], before[:, :], chosen[:, :, :].rearrange("p t e -> p (t e)"), start=True, stop=False)
            M.matmul(psum[:, 1, 8:16], ones[:, :], chosen[:, 0, :], start=False, stop=True)
            M.matmul(psum[:, 1, 16:24], ones[:, :], chosen[:, 0, :], start=True, stop=False)
            M.matmul(psum[:, 1, 16:24], ones[:, :], chosen[:, 1, :], start=False, stop=True).then_inc(pos_done, 1)
            keep_clock(4)

            def expert_pass(half, start):
                e0, s0 = EXPERTS * half, EXPERTS * STEPS * half

                def gather(e):
                    for k in range(KC):
                        for c in range(TT):
                            last = M.matmul(psum[:, 5 + k // 4, (k % 4) * P:(k % 4 + 1) * P], hn[:, c, k * P:(k + 1) * P],
                                            pick[:, e, c, :], start=c == 0, stop=c == TT - 1)
                    last.then_inc(gather_done, 1)

                def spreads():
                    pe.wait_ge(gated_ready, half + 1)
                    for e in range(EXPERTS):
                        for c in range(TT):
                            o = (e % 2) * T + c * P
                            last = M.transpose(psum[:, SPREAD_BANKS[e // 2], o:o + P], gated[:, e, c, :], ident[:, :])
                        if e % 2:
                            last.then_inc(spreadT_done, 1)

                def scatter(i, c):
                    pe.wait_ge(y_e_ready, i + (c + 1))
                    pe.wait_ge(spread_e_ready, i + (c + 1))
                    for t in range(TT):
                        for n in range(2):
                            last = M.matmul(psum[:, (5, 6, 7, 2)[2 * t + n], :], spread_e[:, t * P:(t + 1) * P],
                                            y_e[:, 512 * n:512 * n + 512], start=True, stop=True)
                        last.then_inc(scatter_done if t else tile0_scattered, 1)

                def down(i, j, u, n):
                    pe.wait_ge(eT_ready, i * STEPS + (n + 1))
                    for hf in range(2):
                        w = unit(pe, u + hf, 2, i, PER_EXPERT)
                        for f in range(2):
                            ff = 2 * hf + f
                            for b in range(2):
                                last = mm3(psum[:, 3 + b, :], [a[:, ff, :] for a in (eT_hi, eT_lo)],
                                           [a[:, f, 512 * b:512 * b + 512] for a in w], j == 0 and ff == 0, j == STEPS - 1 and ff == 3)
                        last.then_inc(unit_used, 1)

                def expert(i, first):
                    base = start - 2
                    for j in range(STEPS):
                        n = s0 + j
                        shift = 2 if first and j == 0 else 0
                        if j == 0:
                            pe.wait_ge(sel_ready, i + (e0 + half + 1))
                        for k2, freed in enumerate((e_silu_ready, e_hid_ready)):
                            if not (first and n == 0):
                                pe.wait_ge(freed, i * STEPS + n)
                            if first and j == 0 and k2:
                                spreads()
                                pe.wait_ge(most_ready, 1)
                            for hf in range(2):
                                w = unit(pe, base + 6 * j + shift + 2 * k2 + hf, 4, i, PER_EXPERT)
                                for k in range(4):
                                    kk = 4 * hf + k
                                    last = mm3(psum[:, k2, :], [a[:, kk, :] for a in (sel_hi, sel_lo)],
                                               [a[:, k, :] for a in w], kk == 0, kk == KC - 1)
                                last.then_inc(unit_used, 1)
                        if j == 0 and not first:
                            down(i, STEPS - 1, base + 4, s0 - 1)
                        if j == 1 and not first:
                            scatter(i, e0 - 1)
                        if j == STEPS - 2:
                            gather(i + 1)
                        if j:
                            down(i, j - 1, base + 6 * j + 4, n - 1)
                        if j == 1 and not first:
                            pe.wait_ge(h_added, i + e0)
                        if first and j == 0:
                            pe.wait_ge(spread_ready, 4 * half + 4)
                        pe.wait_ge(e_hid_ready, i * STEPS + (n + 1))
                        for f in range(4):
                            last = M.transpose(psum[:, 2, f * P:(f + 1) * P], e_hid[:, f * P:(f + 1) * P], ident[:, :])
                        last.then_inc(e_T, 1)

                pe.wait_ge(pick_ready, 2 * half + 1)
                gather(0)
                expert(0, True)
                with pe.Fori(1, EXPERTS) as i:
                    expert(i, False)
                down(0, STEPS - 1, start + MOE_UNITS - 2, s0 + EXPERTS * STEPS - 1)
                scatter(0, e0 + EXPERTS - 1)
            expert_pass(0, MOE_U)
            pe.wait_ge(most_ready, 1)
            with pe.If(pe.value_load(most_i[0:1, 0:1], min_val=0, max_val=T) > CAPACITY):
                expert_pass(1, MOE_U + MOE_UNITS)


_INS = ["x", "norm1_g", "w_in", "sgu_norm_g", "sgu_w", "sgu_b", "cmp_pos", "cmp_w1", "cmp_w2", "w_branch", "w_out",
        "norm2_g", "ffn_w_gate", "ffn_w_up", "ffn_w_down", "router_w", "moe_w_gate", "moe_w_up", "moe_w_down",
        "final_norm_g"]


def kernel(**inputs):
    import numpy as _np
    import concourse.bacc as _bacc
    from concourse.bass_utils import run_bass_kernel_spmd as _run

    nc = _bacc.Bacc("TRN2", target_bir_lowering=False, num_devices=1)
    arrays, args = {}, []
    freq = (500000.0 ** (-_np.arange(0, 16, 2, dtype=_np.float32) / 16)).astype(_np.float32)
    ang = _np.arange(T, dtype=_np.float32)[:, None] * freq[None, :]
    table = _np.concatenate([_np.cos(ang), -_np.sin(ang), _np.sin(ang)], axis=1).astype(_np.float32)
    for name in _INS + ["rope"]:
        a = _np.ascontiguousarray(inputs[name]) if name != "rope" else table
        arrays[f"in_{name}"] = a
        args.append(nc.dram_tensor(f"in_{name}", a.shape, mybir.dt.from_np(a.dtype), kind="ExternalInput").ap())
    args.append(nc.dram_tensor("out_0", (1, T, D), F32, kind="ExternalOutput").ap())
    hybrid_trunk(nc, *args)
    r = _run(nc, [arrays], core_ids=[0])
    return r.results[0]["out_0"]
```
